# Optimizing a Trainium2 kernel written in Bass

```python
import math
import jax, jax.numpy as jnp
from jax import lax
import numpy as np

D_MODEL = 1024
BATCH = 1
SEQ = 128
DEPTH = 2
DEC_BATCH = 1
DEC_SEQ = 256
PAST_LEN = 128

GRID_W = 64
N_HEAD_A = 4
HD_A = 64
DV_A = 2 * HD_A
WIDTH_A = N_HEAD_A * DV_A
N_HEAD_B = 4
DK_B = 128
DV_B = 128
WIDTH_B = N_HEAD_B * DV_B
N_HEAD_C = 8
N_KV_C = 2
HD_C = 64
WIDTH_C = N_HEAD_C * HD_C
N_BRANCH = 3
D_FF = 2816
CHUNK = 64
Q_BLOCK = 128
ROPE_THETA = 10000.0
EPS = 1e-6
COL_SIZES = (
    N_HEAD_A * 2 * HD_A, N_HEAD_A * 2 * HD_A, WIDTH_A,
    N_HEAD_B * DK_B, WIDTH_B, N_HEAD_B * DK_B, N_HEAD_B * DK_B, WIDTH_B,
    WIDTH_C, N_KV_C * HD_C, N_KV_C * HD_C,
    N_BRANCH * D_MODEL,
)
COL_SPLITS = tuple(int(s) for s in np.cumsum(COL_SIZES)[:-1])
D_IN = int(sum(COL_SIZES))

kernel_name = 'hybrid_diffusion_prefix_trunk_step'

def rmsnorm(x, g):
    xf = x.astype(jnp.float32)
    xf = xf * lax.rsqrt(jnp.mean(xf * xf, axis=-1, keepdims=True) + EPS)
    return (xf * g.astype(jnp.float32)).astype(x.dtype)

def modulate(x, g, shift, scale):
    return rmsnorm(x, g) * (1 + scale) + shift

def swiglu(h, wg, wu, wd):
    return (jax.nn.silu(h @ wg) * (h @ wu)) @ wd

def axial_rope(x, rows, cols):
    d = x.shape[-1]
    half = d // 2
    quarter = half // 2
    freqs = ROPE_THETA ** (-jnp.arange(quarter, dtype=jnp.float32) / quarter)
    bshape = (x.shape[1],) + (1,) * (x.ndim - 3) + (quarter,)

    def rot(xa, pos):
        ang = (pos.astype(jnp.float32)[:, None] * freqs).reshape(bshape)
        cos, sin = jnp.cos(ang), jnp.sin(ang)
        x1 = xa[..., :quarter].astype(jnp.float32)
        x2 = xa[..., quarter:].astype(jnp.float32)
        return jnp.concatenate([x1 * cos - x2 * sin, x2 * cos + x1 * sin], axis=-1)

    out = jnp.concatenate([rot(x[..., :half], rows), rot(x[..., half:], cols)], axis=-1)
    return out.astype(x.dtype)

def to_query_blocks(q):
    b, t = q.shape[:2]
    return q.reshape((b, t // Q_BLOCK, Q_BLOCK) + q.shape[2:]).swapaxes(0, 1)

def from_query_blocks(o):
    nb, b = o.shape[:2]
    return o.swapaxes(0, 1).reshape((b, nb * o.shape[2]) + o.shape[3:])

def attend_diff(q, k, v, lam):
    scale = q.shape[-1] ** -0.5

    def blk(qi):
        s = jnp.einsum('bqhcd,bkhcd->bhcqk', qi, k).astype(jnp.float32) * scale
        p = jax.nn.softmax(s, axis=-1)
        w = p[:, :, 0] - lam * p[:, :, 1]
        return jnp.einsum('bhqk,bkhv->bqhv', w.astype(v.dtype), v)

    return from_query_blocks(lax.map(blk, to_query_blocks(q)))

def attend_gqa(q, k, v):
    scale = q.shape[-1] ** -0.5

    def blk(qi):
        s = jnp.einsum('bqhgd,bkhd->bhgqk', qi, k).astype(jnp.float32) * scale
        p = jax.nn.softmax(s, axis=-1)
        return jnp.einsum('bhgqk,bkhd->bqhgd', p.astype(v.dtype), v)

    return from_query_blocks(lax.map(blk, to_query_blocks(q)))

def gla_chunkwise(q, k, v, logf, s0):
    b_, t_, h_, _ = q.shape
    dv = v.shape[-1]
    n = t_ // CHUNK

    def to_chunks(a):
        return a.astype(jnp.float32).reshape(b_, n, CHUNK, h_, a.shape[-1]).transpose(1, 0, 3, 2, 4)

    lower = jnp.tril(jnp.ones((CHUNK, CHUNK), dtype=bool))[:, :, None]

    def step(S, inp):
        qc, kc, vc, gc = inp
        b = jnp.cumsum(gc, axis=2)
        o_inter = jnp.einsum('bhtk,bhkv->bhtv', qc * jnp.exp(b), S)
        decay = jnp.exp(jnp.where(lower, b[:, :, :, None, :] - b[:, :, None, :, :], -jnp.inf))
        scores = jnp.einsum('bhtk,bhtsk,bhsk->bhts', qc, decay, kc)
        o = o_inter + jnp.einsum('bhts,bhsv->bhtv', scores, vc)
        b_end = b[:, :, -1:, :]
        S = jnp.exp(b_end[:, :, 0, :])[..., None] * S + jnp.einsum('bhsk,bhsv->bhkv', kc * jnp.exp(b_end - b), vc)
        return S, o

    s_fin, o = lax.scan(step, s0.astype(jnp.float32), (to_chunks(q), to_chunks(k), to_chunks(v), to_chunks(logf)))
    o = o.transpose(1, 0, 3, 2, 4).reshape(b_, t_, h_, dv)
    return o.astype(v.dtype), s_fin.astype(v.dtype)

def hgrn_lower_bounds(raw):
    cs = jnp.cumsum(jax.nn.softmax(raw.astype(jnp.float32), axis=1), axis=1)
    return cs - cs[:, :1]

def hgrn_gate(z, lb):
    zf = z.astype(jnp.float32)
    logf = jnp.logaddexp(jnp.log(lb), jnp.log1p(-lb) + jax.nn.log_sigmoid(zf))
    k = (1 - lb) * jax.nn.sigmoid(-zf)
    shp = z.shape[:2] + (N_HEAD_B, DK_B)
    return k.reshape(shp), logf.reshape(shp)

def token_mixer(h, p, l, ctx, rows, cols):
    b_, t_, _ = h.shape
    (aq, ak, av, bq, bi, bff, bfb, bg, cq, ck, cv, gts) = jnp.split(h @ p['w_in'][l], COL_SPLITS, axis=-1)
    aq = aq.reshape(b_, t_, N_HEAD_A, 2, HD_A)
    ak = ak.reshape(b_, t_, N_HEAD_A, 2, HD_A)
    av = av.reshape(b_, t_, N_HEAD_A, DV_A)
    cq = rmsnorm(cq.reshape(b_, t_, N_HEAD_C, HD_C), p['gqa_qnorm'][l])
    ck = rmsnorm(ck.reshape(b_, t_, N_KV_C, HD_C), p['gqa_knorm'][l])
    cv = cv.reshape(b_, t_, N_KV_C, HD_C)
    bq = jax.nn.silu(bq.reshape(b_, t_, N_HEAD_B, DK_B)) * (DK_B ** -0.5)
    bi = bi.reshape(b_, t_, N_HEAD_B, DV_B)
    lb = hgrn_lower_bounds(p['hgrn_lb'])
    k_f, logf_f = hgrn_gate(bff, lb[0, l])
    k_b, logf_b = hgrn_gate(bfb, lb[1, l])

    if ctx is None:
        s0f = jnp.zeros((b_, N_HEAD_B, DK_B, DV_B), h.dtype)
        s0b = s0f
        a_keys, a_vals, c_keys, c_vals = ak, av, ck, cv
    else:
        ctx_ak, ctx_av, ctx_s, ctx_ck, ctx_cv = ctx
        aq = axial_rope(aq, rows, cols)
        ak = axial_rope(ak, rows, cols)
        cq = axial_rope(cq, rows, cols)
        ck = axial_rope(ck, rows, cols)
        a_keys = jnp.concatenate([ctx_ak.reshape(b_, -1, N_HEAD_A, 2, HD_A), ak], axis=1)
        a_vals = jnp.concatenate([ctx_av, av], axis=1)
        c_keys = jnp.concatenate([ctx_ck, ck], axis=1)
        c_vals = jnp.concatenate([ctx_cv, cv], axis=1)
        s0f, s0b = ctx_s[:, 0], ctx_s[:, 1]

    lam_init = 0.8 - 0.6 * math.exp(-0.3 * l)
    lp = p['diff_lambda'][l].astype(jnp.float32)
    lam = jnp.exp(jnp.sum(lp[0] * lp[1])) - jnp.exp(jnp.sum(lp[2] * lp[3])) + lam_init
    oa = attend_diff(aq, a_keys, a_vals, lam)
    oa = rmsnorm(oa, p['diff_subln'][l]) * (1 - lam_init)

    of, sf = gla_chunkwise(bq, k_f, bi, logf_f, s0f)
    ob, sb = gla_chunkwise(jnp.flip(bq, 1), jnp.flip(k_b, 1), jnp.flip(bi, 1), jnp.flip(logf_b, 1), s0b)
    obr = of + jnp.flip(ob, 1)
    obr = rmsnorm(obr, p['hgrn_gnorm'][l]) * jax.nn.silu(bg.reshape(b_, t_, N_HEAD_B, DV_B))

    oc = attend_gqa(cq.reshape(b_, t_, N_KV_C, N_HEAD_C // N_KV_C, HD_C), c_keys, c_vals)

    ya = oa.reshape(b_, t_, WIDTH_A) @ p['w_branch_a'][l]
    yb = obr.reshape(b_, t_, WIDTH_B) @ p['w_branch_b'][l]
    yc = oc.reshape(b_, t_, WIDTH_C) @ p['w_branch_c'][l]
    g = jax.nn.sigmoid(gts.reshape(b_, t_, N_BRANCH, D_MODEL))
    merged = g[:, :, 0] * ya + g[:, :, 1] * yb + g[:, :, 2] * yc
    out = merged @ p['w_out'][l]
    if ctx is None:
        new_ctx = (ak.reshape(b_, t_, N_HEAD_A, 2 * HD_A), av, jnp.stack([sf, sb], axis=1), ck, cv)
    else:
        new_ctx = None
    return out, new_ctx

def trunk_layer(x, cond, p, l, ctx, rows, cols):
    mod = jax.nn.silu(cond) @ p['ada_w'][l] + p['ada_b'][l]
    m = jnp.split(mod[:, None, :], 9, axis=-1)
    h = modulate(x, p['norm_pre'][l, 0], m[0], m[1])
    y = swiglu(h, p['ffn_gate'][l, 0], p['ffn_up'][l, 0], p['ffn_down'][l, 0])
    x = x + 0.5 * m[2] * rmsnorm(y, p['norm_post'][l, 0])
    h = modulate(x, p['norm_pre'][l, 1], m[3], m[4])
    y, new_ctx = token_mixer(h, p, l, ctx, rows, cols)
    x = x + m[5] * rmsnorm(y, p['norm_post'][l, 1])
    h = modulate(x, p['norm_pre'][l, 2], m[6], m[7])
    y = swiglu(h, p['ffn_gate'][l, 1], p['ffn_up'][l, 1], p['ffn_down'][l, 1])
    x = x + 0.5 * m[8] * rmsnorm(y, p['norm_post'][l, 2])
    return x, new_ctx

def setup_inputs(seed: int = 0) -> dict:
    key = jax.random.key(seed)
    ks = jax.random.split(key, 32)
    nrm = jax.random.normal
    f32 = jnp.float32
    d = D_MODEL
    return {
        'x_prompt': nrm(ks[0], (BATCH, SEQ, d), f32),
        'x_sample': nrm(ks[1], (DEC_BATCH, DEC_SEQ, d), f32),
        'c': nrm(ks[2], (DEC_BATCH, d), f32),
        'cache_a_k': nrm(ks[3], (DEC_BATCH, DEPTH, PAST_LEN, N_HEAD_A, 2 * HD_A), f32),
        'cache_a_v': nrm(ks[4], (DEC_BATCH, DEPTH, PAST_LEN, N_HEAD_A, DV_A), f32),
        'state_hgrn': nrm(ks[5], (DEC_BATCH, DEPTH, 2, N_HEAD_B, DK_B, DV_B), f32),
        'cache_c_k': nrm(ks[6], (DEC_BATCH, DEPTH, PAST_LEN, N_KV_C, HD_C), f32),
        'cache_c_v': nrm(ks[7], (DEC_BATCH, DEPTH, PAST_LEN, N_KV_C, HD_C), f32),
        'c_ctx': nrm(ks[8], (d,), f32),
        'ada_w': nrm(ks[9], (DEPTH, d, 9 * d), f32) * d ** -0.5,
        'ada_b': 0.02 * nrm(ks[10], (DEPTH, 9 * d), f32),
        'norm_pre': 1.0 + 0.05 * nrm(ks[11], (DEPTH, 3, d), f32),
        'norm_post': 1.0 + 0.05 * nrm(ks[12], (DEPTH, 3, d), f32),
        'ffn_gate': nrm(ks[13], (DEPTH, 2, d, D_FF), f32) * d ** -0.5,
        'ffn_up': nrm(ks[14], (DEPTH, 2, d, D_FF), f32) * d ** -0.5,
        'ffn_down': nrm(ks[15], (DEPTH, 2, D_FF, d), f32) * D_FF ** -0.5,
        'w_in': nrm(ks[16], (DEPTH, d, D_IN), f32) * d ** -0.5,
        'diff_lambda': 0.1 * nrm(ks[17], (DEPTH, 4, HD_A), f32),
        'diff_subln': 1.0 + 0.05 * nrm(ks[18], (DEPTH, DV_A), f32),
        'hgrn_lb': 0.5 * nrm(ks[19], (2, DEPTH, N_HEAD_B * DK_B), f32),
        'hgrn_gnorm': 1.0 + 0.05 * nrm(ks[20], (DEPTH, DV_B), f32),
        'gqa_qnorm': 1.0 + 0.05 * nrm(ks[21], (DEPTH, HD_C), f32),
        'gqa_knorm': 1.0 + 0.05 * nrm(ks[22], (DEPTH, HD_C), f32),
        'w_branch_a': nrm(ks[23], (DEPTH, WIDTH_A, d), f32) * WIDTH_A ** -0.5,
        'w_branch_b': nrm(ks[24], (DEPTH, WIDTH_B, d), f32) * WIDTH_B ** -0.5,
        'w_branch_c': nrm(ks[25], (DEPTH, WIDTH_C, d), f32) * WIDTH_C ** -0.5,
        'w_out': nrm(ks[26], (DEPTH, d, d), f32) * d ** -0.5,
    }

def reference(x_prompt, x_sample, c, cache_a_k, cache_a_v, state_hgrn, cache_c_k, cache_c_v, c_ctx,
              ada_w, ada_b, norm_pre, norm_post, ffn_gate, ffn_up, ffn_down, w_in, diff_lambda, diff_subln,
              hgrn_lb, hgrn_gnorm, gqa_qnorm, gqa_knorm, w_branch_a, w_branch_b, w_branch_c, w_out):
    p = {
        'ada_w': ada_w, 'ada_b': ada_b, 'norm_pre': norm_pre, 'norm_post': norm_post,
        'ffn_gate': ffn_gate, 'ffn_up': ffn_up, 'ffn_down': ffn_down, 'w_in': w_in,
        'diff_lambda': diff_lambda, 'diff_subln': diff_subln, 'hgrn_lb': hgrn_lb, 'hgrn_gnorm': hgrn_gnorm,
        'gqa_qnorm': gqa_qnorm, 'gqa_knorm': gqa_knorm, 'w_branch_a': w_branch_a, 'w_branch_b': w_branch_b,
        'w_branch_c': w_branch_c, 'w_out': w_out,
    }
    n_lat = x_sample.shape[1]
    rows_n = n_lat // GRID_W
    rows = jnp.repeat(jnp.arange(rows_n, dtype=jnp.int32), GRID_W)
    cols = jnp.tile(jnp.arange(GRID_W, dtype=jnp.int32), rows_n)

    xp, xs = x_prompt, x_sample
    new_ak, new_av, new_s, new_ck, new_cv = [], [], [], [], []
    for l in range(DEPTH):
        xp, (ak_l, av_l, s_l, ck_l, cv_l) = trunk_layer(xp, c_ctx[None, :], p, l, None, None, None)
        new_ak.append(ak_l)
        new_av.append(av_l)
        new_s.append(s_l)
        new_ck.append(ck_l)
        new_cv.append(cv_l)
        ctx_l = (cache_a_k[:, l], cache_a_v[:, l], state_hgrn[:, l], cache_c_k[:, l], cache_c_v[:, l])
        xs, _ = trunk_layer(xs, c, p, l, ctx_l, rows, cols)

    new_a_k = jnp.stack(new_ak, axis=1)
    new_a_v = jnp.stack(new_av, axis=1)
    new_hgrn = jnp.stack(new_s, axis=1)
    new_c_k = jnp.stack(new_ck, axis=1)
    new_c_v = jnp.stack(new_cv, axis=1)
    return (xp, xs, new_a_k, new_a_v, new_hgrn, new_c_k, new_c_v)


_drawn_inputs = setup_inputs


def setup_inputs(seed=0):
    import zlib

    import numpy as np

    out = dict(_drawn_inputs(seed))
    spreads = {}
    factors = {'state_hgrn': 8.0, 'gqa_qnorm': 8.0}
    for name, (base, spread) in spreads.items():
        noise = np.random.default_rng([zlib.crc32(name.encode()), seed]).standard_normal(out[name].shape)
        drawn = base * np.exp(spread * noise) if base else spread * noise
        out[name] = __import__('jax').numpy.asarray(drawn.astype(out[name].dtype))
    for name, factor in factors.items():
        out[name] = (out[name] * factor).astype(out[name].dtype)
    return out
```

```python
from collections import namedtuple
from contextlib import ExitStack
import math

import numpy as np
import concourse.bass as bass
from concourse import mybir

D, SEQ, LAT, DEPTH, PAST = 1024, 128, 256, 2, 128
T = SEQ + LAT
NB = T // 128
KT = D // 128
FF = 2816
FT = FF // 128
HA, HB, HC, KVC = 4, 4, 8, 2
GRID_W = 64
EPS = 1e-6
THETA = 10000.0
MODS = 9
MOD_TILES = MODS * KT
LAM_INIT = [0.8 - 0.6 * math.exp(-0.3 * l) for l in range(DEPTH)]
SLOTS = 4
AQ, AK, AV, BQ, BI, BFF, BFB, BG, CQ, CK, CV = 0, 4, 8, 12, 16, 20, 24, 28, 32, 36, 37
P_TILES = 38
GATE_COL = P_TILES * 128
LEVELS = [128, 64, 32, 16, 8, 4, 2]
V_PRE, V_POST, V_ROWS = MOD_TILES, MOD_TILES + 3 * KT, MOD_TILES + 6 * KT
M_CTX, M_C, M_LB, M_SUB, M_GN, M_QN, M_KN, M_ROWS = 0, 8, 16, 32, 34, 36, 38, 40
C_ID, C_ONE, C_HEAD, C_SWAP, C_DUP, C_COS, C_SIN, C_LAM, C_N = 0, 128, 256, 384, 512, 768, 1024, 1280, 1284


Unit = namedtuple("Unit", "slot nk width src dest part k0 first last rhs tag split")

TURNS = None


class Seen:

    def __init__(self, turns, learn):
        self.n, self.turns, self.learn, self.loops = {}, turns, learn, []

    def start(self, key, value):
        self.n[key] = (value, {})

    def next(self, key, count=1):
        const, regs = self.n.get(key, (0, {}))
        self.n[key] = (const + count, regs)
        return self.value(key)

    def value(self, key, back=0):
        const, regs = self.n[key]
        out = const - back
        for reg, per in regs.values():
            if per:
                out = reg * per + out
        return out

    def enter(self, name, reg):
        per = self.turns.get(name, {})
        self.loops.append((name, dict(self.n)))
        for key in set(self.n) | set(per):
            const, regs = self.n.get(key, (0, {}))
            self.n[key] = (const, {**regs, name: (reg, per.get(key, 0))})

    def leave(self, turns):
        name, before = self.loops.pop()
        per = self.turns.setdefault(name, {})
        for key, (const, regs) in list(self.n.items()):
            const0, regs0 = before.get(key, (0, {}))
            step = const - const0
            if self.learn:
                per[key] = step
            assert step == per.get(key, 0), (name, key, step, per.get(key, 0))
            self.n[key] = (const0 + turns * step, regs0)


def build(nc, io, out, turns, learn=False):
    f32, f32r, u8 = mybir.dt.float32, mybir.dt.float32r, mybir.dt.uint8
    ALU, ACT, AX = mybir.AluOpType, mybir.ActivationFunctionType, mybir.AxisListType
    MUL, ADD, SUB = ALU.mult, ALU.add, ALU.subtract
    ds = bass.ds

    base = 16512

    def at(name, shape, dt, offset):
        size = (int(np.prod(shape[1:])) * (1 if dt == u8 else 4) + 31) // 32 * 32
        return nc.alloc_sbuf_tensor_at(name, shape, dt, offset=offset), offset + size

    x, o = at("x", [128, KT, T], f32, base)
    h_hi, o = at("h_hi", [128, KT, T], f32r, o)
    h_lo, o = at("h_lo", [128, KT, T], f32r, o)
    raw, o = at("raw", [128, SLOTS, 1024], f32, o)
    w_hi, o = at("w_hi", [128, SLOTS, 1024], f32r, o)
    w_lo, o = at("w_lo", [128, SLOTS, 1024], f32r, o)
    R = o
    act_hi, o = at("act_hi", [128, FT, T], f32r, R)
    act_lo, R_END = at("act_lo", [128, FT, T], f32r, o)
    proj, r = at("proj", [128, P_TILES, T], f32, R)
    s_in, r = at("s_in", [128, 2, HB, 128], f32, r)
    s_mid, r = at("s_mid", [128, 2, HB, 128], f32, r)
    assert r <= R_END
    mg_hi, r = at("mg_hi", [128, KT, T], f32r, R)
    mg_lo, r = at("mg_lo", [128, KT, T], f32r, r)
    gate = []
    for b in range(3):
        g, r = at(f"gate{b}", [128, 2, T], f32, r)
        gate.append(g)
    acc, r = at("acc", [128, 2, T], f32, r)
    acc2, r = at("acc2", [128, 2, T], f32, r)
    Y = R_END
    y, o = at("y", [128, KT, T], f32, Y)
    sq, o = at("sq", [128, KT, T], f32, o)
    silu, o = at("silu", [128, 2, T], f32, o)
    prod, o = at("prod", [128, 2, T], f32, o)
    Y_END = Y + 36864
    assert o <= Y_END
    br_hi, o = at("br_hi", [128, 12, T], f32r, Y)
    br_lo, o = at("br_lo", [128, 12, T], f32r, o)
    assert o == Y_END
    rows, o = at("rows", [128, 3, 128], f32, Y)
    x_rows, o = at("x_rows", [128, NB, D], f32, o)
    lam_in, o = at("lam_in", [128, DEPTH, 4, 64], f32, o)
    lam_p, o = at("lam_p", [128, DEPTH * 2, 64], f32, o)
    mask_f, o = at("mask_f", [128, 2, len(LEVELS), 128], f32, o)
    ctx_k, o = at("ctx_k", [128, 512], f32, Y)
    ctx_v, o = at("ctx_v", [128, 512], f32, o)
    ctx_kT, o = at("ctx_kT", [128, HA, 128], f32, o)
    v_nat, o = at("v_nat", [128, NB, 512], f32, o)
    k_nat, o = at("k_nat", [128, 512], f32, o)
    p = []
    for b in range(2):
        t_, o = at(f"p{b}", [128, 2, T], f32, o)
        p.append(t_)
    comb, o = at("comb", [128, T], f32, o)
    pT, o = at("pT", [128, 2, T], f32, o)
    rope_t, o = at("rope_t", [128, 4, LAT], f32, o)
    rope_u, o = at("rope_u", [128, 4, LAT], f32, o)
    assert o <= Y_END
    ctx_ck, o = at("ctx_ck", [128, 128], f32, Y)
    ctx_cv, o = at("ctx_cv", [128, 128], f32, o)
    c_kT, o = at("c_kT", [128, PAST + T], f32, o)
    c_kd, o = at("c_kd", [128, KVC, PAST + T], f32, o)
    c_nat, o = at("c_nat", [128, 512], f32, o)
    c_vd, o = at("c_vd", [128, KVC, 4, 2, 64], f32, o)
    assert o <= Y + 14 * 1024
    c_sq, o = at("c_sq", [128, 5, T], f32, Y + 18432)
    c_rt, o = at("c_rt", [128, 5, T], f32, o)
    assert o <= Y_END
    b_f, o = at("b_f", [128, HB * T], f32, Y)
    b_b, o = at("b_b", [128, HB * T], f32, o)
    scores, o = at("scores", [128, HB * T], f32, o)
    v_b, o = at("v_b", [128, NB, HB, 128], f32, o)
    W0 = o
    dec = []
    for b in range(2):
        t_, o = at(f"dec{b}", [128, 2 * T], f32, o)
        dec.append(t_)
    lev = []
    for b in range(2):
        t_, o = at(f"lev{b}", [128, 2 * T], f32, o)
        lev.append(t_)
    assert o == Y_END
    k_sum, _ = at("k_sum", [128, HB * T], f32, W0)
    q_st, o = at("q_st", [128, 2, HB, LAT], f32, W0)
    k_st, o = at("k_st", [128, HB, 256], f32, o)
    assert o == Y_END
    o_sq, o = at("o_sq", [128, HB, T], f32, W0)
    o_rt, o = at("o_rt", [128, HB, T], f32, o)
    k_bn, r = [], 0
    for b in range(2):
        t_, r = at(f"k_bn{b}", [128, HB, 2, 128], f32, R + (BFF + 4 * b) * T * 4)
        s_, r = at(f"s_out{b}", [128, HB, 128], f32, r)
        k_bn.append((t_, s_))
    o = Y_END
    con, o = at("con", [128, C_N], f32, o)
    masks, o = at("masks", [128, 2, len(LEVELS), 128], u8, o)
    o = (o + 31) // 32 * 32
    reset, o = at("reset", [128, HB * T], f32, o)
    vec, o = at("vec", [128, DEPTH, V_ROWS, 2], f32, o)
    misc, o = at("misc", [128, M_ROWS], f32, o)
    mod, o = at("mod", [128, MOD_TILES + 2 * KT, 2], f32, o)
    y_sum, o = at("y_sum", [128, T], f32, o)
    tick, o = at("tick", [128, 1], f32, o)
    mod_t, o = at("mod_t", [128, 2, 2], f32, o)
    c4, o = at("c4", [128, KT, 4], f32r, o)
    c_act, o = at("c_act", [128, KT, 2], f32, o)
    mA, o = at("mA", [128, KT, 2], f32, o)
    mB, o = at("mB", [128, KT, 2], f32, o)
    mG, o = at("mG", [128, KT, 2], f32, o)
    root, o = at("root", [128, T], f32, o)
    rinv, o = at("rinv", [128, T], f32, o)
    eps, o = at("eps", [128, 1], f32, o)
    lam_s, o = at("lam_s", [128, DEPTH, 2], f32, o)
    neg_lam, o = at("neg_lam", [128, DEPTH], f32, o)
    lb, o = at("lb", [128, DEPTH, 2, HB], f32, o)
    omlb, o = at("omlb", [128, DEPTH, 2, HB], f32, o)
    lb_d, o = at("lb_d", [128, 2, HB], f32, o)
    sub_g, o = at("sub_g", [128, DEPTH], f32, o)
    qn_g, o = at("qn_g", [128, DEPTH], f32, o)
    one_l, o = at("one_l", [128, 8], f32, o)
    lbl, o = at("lbl", [128, 2, 2, HB], f32, o)
    nmax, o = at("nmax", [128, 2, 2], f32, o)
    esum, o = at("esum", [128, 2, 2], f32, o)
    rsum, o = at("rsum", [128, 2], f32, o)
    ends, o = at("ends", [128, 2, HB * NB], f32, o)
    dend, o = at("dend", [128, 2, HB], f32, o)
    assert o <= nc.sbuf_usable_end, (o, nc.sbuf_usable_end)

    ident, ones = con[:, C_ID:C_ID + 128], con[:, C_ONE:C_ONE + 128]
    head_ones, swap = con[:, C_HEAD:C_HEAD + 128], con[:, C_SWAP:C_SWAP + 128]

    with ExitStack() as ctx:
        def pb(name, shape):
            return ctx.enter_context(nc.psum_tensor(name, shape, f32))

        X = [pb("X0", [128, 2, 512]), pb("X1", [128, 2, 512])]
        Ab = pb("Ab", [128, 512])
        S5, S6, S7 = pb("S5", [128, 512]), pb("S6", [128, 512]), pb("S7", [128, 512])

        def sem(name):
            return ctx.enter_context(nc.semaphore(name))

        loaded = [sem(f"loaded{s}") for s in range(SLOTS)]
        hi_ready = [sem(f"hi_ready{s}") for s in range(SLOTS)]
        lo_ready = [sem(f"lo_ready{s}") for s in range(SLOTS)]
        unit_done = [sem(f"unit_done{s}") for s in range(SLOTS)]
        x_free = [sem("x0_free"), sem("x1_free")]
        ada_free = sem("ada_free")
        names = ("const_in mask_in rows_in lam_in_s x_in rows_turned vec_ready c_ready c4_ready x_turned x_copied x_ready "
                 "x_sq_ready y_sq_ready sum_ready root_ready norm_ready hh_ready h_ready silu_ready act_ready "
                 "dve_step act_step credits "
                 "proj_ready ctx_in nat_ready nat_copied nat_out swap_ready rope_done scores_ready max_ready "
                 "probs_ready comb_ready turned_ready turned_copied out_ready out_taken "
                 "o_sq_ready o_sum_ready o_root_ready br_ready br_hi_ready split_ready "
                 "c_sq_ready c_sum_ready c_root_ready c_norm_done dup_ready dup_copied "
                 "rec_gate_ready f_ready logf_ready diag_in lev_free dec_ready exp_ready lev_ready lev_prod lev_taken "
                 "st_in st_exp q_dec_ready k_dec_ready kn_ready kn_copied st_ready st_taken o_ready o_taken bg_ready "
                 "sig_ready acc_ready mg_ready y_turned y_out_ready stored_a stored_c stored_s stored_y s_in_s ctx_c_in v_ready c_keys_ready").split()
        S = {n: sem(n) for n in names}
        block = ctx.enter_context(nc.Block())

        ITEMS = [(d, l, half) for d in range(2) for l in range(len(LEVELS)) for half in range(2)]
        STEPS = [(h, b) for h in range(4) for b in range(NB)]

        def keys_of(b):
            return [0] if b == 0 else [3, 1, 2]

        def weight(w, L, r0, nk, col, width, f=None):
            v = w[ds(L, 1), r0:r0 + nk * 128, ds(col, width)] if f is None else \
                w[ds(L, 1), f, r0:r0 + nk * 128, ds(col, width)]
            return v.rearrange("l (k p) c -> p (l k) c", p=128)

        def number(units):
            out_ = []
            for n, u in enumerate(units):
                out_.append(u._replace(slot=n % SLOTS))
            return out_

        def halves(src, dest, rhs, tag, tiles=KT):
            out_ = []
            for k0 in range(0, tiles, 4):
                nk = min(4, tiles - k0)
                out_.append(Unit(0, nk, 256, src(k0, nk), dest, 0, k0, k0 == 0, k0 + nk == tiles, rhs, tag, "pool"))
            return out_

        def ada(layer, unit, tag, split=("dve", "dve")):
            return [Unit(0, KT, 128,
                         (lambda j: lambda L, i: weight(io["ada_w"], layer(L), 0, KT, unit(i) * 256 + j * 128, 128))(j),
                         "ada", j, 0, j == 0, j == 1, "c", tag, split[j]) for j in range(2)]

        def between(units, riders):
            out_ = []
            for n, u in enumerate(units):
                out_ += [u] + riders[n:n + 1]
            return out_

        this, after = (lambda L: L), (lambda L: DEPTH - 1)

        def up_units(f):
            def src(w):
                return lambda k0, nk: lambda L, i: weight(io[w], L, k0 * 128, nk, i * 256, 256, f)
            return number(halves(src("ffn_gate"), 0, "h", "gate") + halves(src("ffn_up"), 1, "h", "up"))

        def down_units(f):
            u = []
            for j in range(2):
                d = halves((lambda j: lambda k0, nk: lambda L, i:
                            weight(io["ffn_down"], L, k0 * 128, nk, i * 512 + j * 256, 256, f))(j), j, "act", ("down", j), FT)
                layer, one, two, at_ = (this, 8, 12, 12) if f == 0 else (after, 32, 0, 36)
                a = [ada(this, (lambda j: lambda i: i * 2 + one + j)(j), ("mod", one + j, 2))]
                a += [ada(layer, (lambda m: lambda i: i * 4 + two + m)(2 * j + r), ("mod", at_ + 2 * j + r, 4))
                      for r in range(2)]
                u += between(d, a[0] + a[1] + a[2])
            return number(u)

        def in_src(col):
            return lambda k0, nk: lambda L, i: weight(io["w_in"], L, k0 * 128, nk, col(i), 256)

        def proj_units():
            u = []
            riders = [a for j in range(2)
                      for a in ada(this, (lambda j: lambda i: i * 2 + 20 + j)(j), ("mod", 20 + j, 2))]
            for j in range(4):
                u += between(halves(in_src((lambda j: lambda i: i * 1024 + j * 256)(j)), j % 2, "h", ("proj", j)),
                             riders[j:j + 1])
            return number(u)

        def proj_tail_units():
            u = []
            for j in range(3):
                u += halves(in_src((lambda j: lambda i: 4096 + j * 256)(j)), j % 2, "h", ("tail", j))
            return number(u)

        def merge_units():
            u = []
            riders = ada(this, lambda i: i + 28, ("mod", 28, 1))
            for b in range(3):
                u += between(halves(in_src((lambda b: lambda i: i * 256 + GATE_COL + b * D)(b)), b % 2, "h", ("g", b)),
                             riders[b:b + 1])
            for b, w in enumerate(("w_branch_a", "w_branch_b", "w_branch_c")):
                u += halves((lambda w: lambda k0, nk: lambda L, i: weight(io[w], L, k0 * 128, nk, i * 256, 256))(w),
                            (b + 1) % 2, ("br", b), ("b", b), 4)
            return number(u)

        def out_units():
            u = []
            for j in range(2):
                u += halves((lambda j: lambda k0, nk: lambda L, i:
                             weight(io["w_out"], L, k0 * 128, nk, i * 512 + j * 256, 256))(j), j, "mg", ("out", j))
            return number(u)

        def first_units():
            return number(ada(lambda L: 0, lambda i: i * 2, ("mod", 36, 2), ("pool", "dve")) +
                          ada(lambda L: 0, lambda i: i * 2 + 1, ("mod", 37, 2), ("pool", "dve")))

        def slot(t, u):
            return t[:, u.slot, 0:u.nk * u.width]

        @block.sync
        def _(sp):
            seen = Seen(turns.setdefault("SP", {}), learn)

            def stream(units, L, i):
                for u in units:
                    sp.wait_ge(lo_ready[u.slot], seen.next(("split", u.slot)))
                    sp.dma_start(slot(raw, u).rearrange("p (k c) -> p k c", c=u.width), u.src(L, i)) \
                        .then_inc(loaded[u.slot], 16)

            def loop(name, count, units, L):
                with sp.Fori(0, count) as i:
                    seen.enter(name, i)
                    stream(units, L, i)
                    seen.leave(count)

            sp.dma_start(con[:, :], io["consts"]).then_inc(S["const_in"], 16)
            sp.dma_start(rows[0:V_ROWS, 0:DEPTH, :], io["vec_rows"].rearrange("l r c -> r l c")).then_inc(S["rows_in"], 16)
            for name, r0, n, c0, w in (("c_ctx", M_CTX, KT, 0, 128), ("c", M_C, KT, 0, 128), ("hgrn_lb", M_LB, 16, 0, 128),
                                       ("diff_subln", M_SUB, 2, 0, 128), ("hgrn_gnorm", M_GN, 2, 0, 128),
                                       ("gqa_qnorm", M_QN, 2, 0, 64), ("gqa_qnorm", M_QN, 2, 64, 64),
                                       ("gqa_knorm", M_KN, 2, 0, 64), ("gqa_knorm", M_KN, 2, 64, 64)):
                sp.dma_start(rows[r0:r0 + n, 2, c0:c0 + w], io[name]).then_inc(S["rows_in"], 16)
            sp.dma_start(x_rows[:, 0, :], io["x_prompt"][0]).then_inc(S["x_in"], 16)
            sp.dma_start(x_rows[:, 1:3, :], io["x_sample"][0].rearrange("(b p) c -> p b c", p=128)).then_inc(S["x_in"], 16)
            sp.dma_start(mask_f[:, :, :, :], io["masks"]).then_inc(S["mask_in"], 16)
            sp.dma_start(lam_in[:, :, :, :], io["diff_lambda"].partition_broadcast(128)).then_inc(S["lam_in_s"], 16)
            loop("first", 4, first_units(), 0)
            with sp.Fori(0, DEPTH) as L:
                seen.enter("layer", L)
                for f in range(2):
                    loop(f"up{f}", 11, up_units(f), L)
                    loop(f"down{f}", 2, down_units(f), L)
                    if f == 0:
                        loop("proj", 4, proj_units(), L)
                        stream(proj_tail_units(), L, 0)
                        loop("merge", 4, merge_units(), L)
                        loop("out", 2, out_units(), L)
                seen.leave(DEPTH)

        @block.gpsimd
        def _(pool):
            seen = Seen(turns.setdefault("Pool", {}), learn)

            def low_part(u):
                there = seen.next(("hi", u.slot))
                if u.split == "pool":
                    pool.wait_ge(hi_ready[u.slot], there)
                    nc.gpsimd.tensor_tensor(slot(w_lo, u), slot(raw, u), slot(w_hi, u), SUB).then_inc(lo_ready[u.slot], 1)

            def stream(units):
                for u in units:
                    low_part(u)

            def loop(name, count, units):
                with pool.Fori(0, count) as i:
                    seen.enter(name, i)
                    stream(units)
                    seen.leave(count)

            def loop_after_pre(name, count, units):
                stream(units[:SLOTS])
                for c in range(4):
                    pool.wait_ge(S["hh_ready"], seen.next("hh_ready"))
                    t = slice(2 * c, 2 * c + 2)
                    nc.gpsimd.tensor_tensor(h_lo[:, t, :], sq[:, t, :], h_hi[:, t, :], SUB).then_inc(S["h_ready"], 1)
                with pool.Fori(0, count - 1) as i:
                    seen.enter(name, i)
                    stream(units[SLOTS:] + units[:SLOTS])
                    seen.leave(count - 1)
                stream(units[SLOTS:])

            def rec_decays():
                pool.wait_ge(S["lev_prod"], seen.next("lev_prod"))
                seen.next("lev_prod", len(ITEMS))
                for n, (d, l, half) in enumerate(ITEMS):
                    par, b = LEVELS[l], LEVELS[l] // 2
                    src = (b_f, b_b)[d][:, half * 768:half * 768 + 768].rearrange("p (n c) -> p n c", c=par)
                    dst = dec[n % 2][:, :].rearrange("p (n c) -> p n c", c=par)
                    mid = src[:, :, b - 1:b] if d == 0 else src[:, :, b:b + 1]
                    mid = mid.broadcast_to([128, 768 // par, b])
                    if n >= 2:
                        pool.wait_ge(S["lev_ready"], seen.next("lev_ready"))
                    if d == 0:
                        nc.gpsimd.tensor_tensor(dst[:, :, 0:b], mid, src[:, :, 0:b], SUB)
                        nc.gpsimd.tensor_tensor(dst[:, :, b:], src[:, :, b:], mid, SUB).then_inc(S["dec_ready"], 1)
                    else:
                        nc.gpsimd.tensor_tensor(dst[:, :, 0:b], mid, src[:, :, 0:b], SUB)
                        nc.gpsimd.tensor_tensor(dst[:, :, b:], src[:, :, b:], mid, SUB).then_inc(S["dec_ready"], 1)
                seen.next("lev_ready", 2)

            for s in range(SLOTS):
                pool.sem_inc(lo_ready[s], 1)
            loop("first", 4, first_units())
            with pool.Fori(0, DEPTH) as L:
                seen.enter("layer", L)
                for f in range(2):
                    loop_after_pre(f"up{f}", 11, up_units(f))
                    loop(f"down{f}", 2, down_units(f))
                    if f == 0:
                        loop_after_pre("proj", 4, proj_units())
                        stream(proj_tail_units())
                        rec_decays()
                        loop("merge", 4, merge_units())
                        loop("out", 2, out_units())
                seen.leave(DEPTH)

        @block.tensor
        def _(pe):
            seen = Seen(turns.setdefault("PE", {}), learn)
            for s in range(SLOTS):
                seen.start(("lo", s), 1)
            seen.start("act_ready", 1)
            seen.start("mg_ready", 1)

            RHS = {"h": (h_hi, h_lo, 0), "act": (act_hi, act_lo, 0), "mg": (mg_hi, mg_lo, 0)}
            for b in range(3):
                RHS["br", b] = (br_hi, br_lo, 4 * b)

            def stream(units):
                for u in units:
                    pe.wait_ge(lo_ready[u.slot], seen.next(("lo", u.slot)))
                    hi, lo = (slot(t, u).rearrange("p (k c) -> p k c", c=u.width) for t in (w_hi, w_lo))
                    if u.dest == "ada":
                        if u.first:
                            pe.wait_ge(ada_free, seen.next("ada_free"))
                        for k in range(u.nk):
                            for n, w in enumerate((hi, lo)):
                                mm = nc.tensor.matmul(Ab[:, 4 * u.part:4 * u.part + 4], w[:, k, :], c4[:, k, :],
                                                      start=k + n == 0, stop=k == u.nk - 1 and n == 1)
                    else:
                        if u.first:
                            pe.wait_ge(x_free[u.dest], seen.next(("xf", u.dest)))
                        r_hi, r_lo, r0 = RHS[u.rhs]
                        for m in range(2):
                            for k in range(u.nk):
                                kk = r0 + u.k0 + k
                                for n, (w, r_) in enumerate(((hi, r_hi), (hi, r_lo), (lo, r_hi))):
                                    mm = nc.tensor.matmul(X[u.dest][:, m, 0:T], w[:, k, m * 128:m * 128 + 128],
                                                          r_[:, kk, :], start=u.first and k + n == 0,
                                                          stop=u.last and k == u.nk - 1 and n == 2)
                    mm.then_inc(unit_done[u.slot], 1)

            def loop(name, count, units, moving=None):
                with pe.Fori(0, count) as i:
                    seen.enter(name, i)
                    for n, u in enumerate(units):
                        if moving and n < len(moving) - 1:
                            pe.wait_ge(S[moving[0]], moving[1 + n])
                        stream([u])
                    seen.leave(count)

            def y_sums():
                pe.wait_ge(S["y_sq_ready"], seen.next("y_sq_ready", 4))
                nc.tensor.matmul(S5[:, 0:T], ones, y_sum[:, :], start=True, stop=True).then_inc(S["sum_ready"], 1)

            def sums(ready):
                for c in range(4):
                    pe.wait_ge(S[ready], seen.next(ready))
                    for k in (2 * c, 2 * c + 1):
                        mm = nc.tensor.matmul(S5[:, 0:T], ones, sq[:, k, :], start=k == 0, stop=k == KT - 1)
                mm.then_inc(S["sum_ready"], 1)

            def pre():
                sums("x_sq_ready")
                half = seen.next("h_ready", 2)
                return "h_ready", half, seen.next("h_ready", 2)

            def head_sums():
                pe.wait_ge(S["o_sq_ready"], seen.next("o_sq_ready"))
                for h in range(4):
                    mm = nc.tensor.matmul(X[h // 2][:, h % 2, 0:T], ones, o_sq[:, h, :], start=True, stop=True)
                mm.then_inc(S["o_sum_ready"], 1)

            def turn_tokens(tile0, dests):
                for b, d in dests:
                    for h in range(4):
                        mm = nc.tensor.transpose(d[:, h * 128:h * 128 + 128],
                                                 proj[:, tile0 + h, b * 128:b * 128 + 128], ident)
                return mm

            def swaps(tile0, tiles, xb):
                for t in range(tiles):
                    mm = nc.tensor.matmul(X[xb][:, t // 2, t % 2 * 256:t % 2 * 256 + 256], swap,
                                          proj[:, tile0 + t, SEQ:T], start=True, stop=True)
                mm.then_inc(S["swap_ready"], 1)

            def attention(kind):
                def keys(h, b, c):
                    q = slice(64 * c, 64 * c + 64)
                    if kind == "a":
                        return [(0, proj[q, AK + h, 0:SEQ])] if b == 0 else \
                            [(0, ctx_kT[q, h, :]), (PAST, proj[q, AK + h, SEQ:T])]
                    kd = c_kd[q, h // 2, :]
                    return [(0, kd[:, PAST:PAST + SEQ])] if b == 0 else [(0, kd[:, 0:PAST]), (PAST, kd[:, PAST + SEQ:])]

                def score(n):
                    h, b = STEPS[n]
                    if n >= 2:
                        pe.wait_ge(S["probs_ready"], seen.next("probs_ready"))
                    for c in range(2):
                        for at_, k in keys(h, b, c):
                            mm = nc.tensor.matmul(X[n % 2][:, c, at_:at_ + k.shape[-1]],
                                                  proj[64 * c:64 * c + 64, (AQ if kind == "a" else CQ) + h,
                                                       b * 128:b * 128 + 128], k, start=True, stop=True)
                    mm.then_inc(S["scores_ready"], 1)

                def turn(n):
                    h, b = STEPS[n]
                    pe.wait_ge(S["comb_ready"], seen.next("comb_ready"))
                    if n >= 1:
                        pe.wait_ge(S["turned_copied"], seen.next("turned_copied"))
                    for c in range(1 if kind == "a" else 2):
                        for kb in range(len(keys_of(b))):
                            src = comb[:, kb * 128:kb * 128 + 128] if kind == "a" else \
                                p[n % 2][:, c, kb * 128:kb * 128 + 128]
                            mm = nc.tensor.transpose((S5, S6)[c][:, kb * 128:kb * 128 + 128], src, ident)
                    mm.then_inc(S["turned_ready"], 1)

                def mix(n):
                    h, b = STEPS[n]
                    if n == len(STEPS) - 1:
                        pe.wait_ge(S["turned_copied"], seen.next("turned_copied"))
                    if n >= 1:
                        pe.wait_ge(S["out_taken"], seen.next("out_taken"))
                    kbs = keys_of(b)
                    for c in range(1 if kind == "a" else 2):
                        for j, kb in enumerate(kbs):
                            if kind == "a":
                                v = ctx_v[:, h * 128:h * 128 + 128] if kb == 3 else v_nat[:, kb, h * 128:h * 128 + 128]
                            else:
                                v = c_vd[:, h // 2, kb, :, :].rearrange("p a c -> p (a c)")
                            mm = nc.tensor.matmul(S7[:, c * 128:c * 128 + 128], v, pT[:, c, j * 128:j * 128 + 128],
                                                  start=j == 0, stop=j == len(kbs) - 1)
                    mm.then_inc(S["out_ready"], 1)

                score(0)
                for n in range(len(STEPS) + 1):
                    if n + 1 < len(STEPS):
                        score(n + 1)
                    if n < len(STEPS):
                        turn(n)
                    if n >= 1:
                        mix(n - 1)
                seen.next("probs_ready", 2)
                seen.next("out_taken")

            def block_out(n):
                return X[n // 8][:, n % 8 // 4, n % 4 * 128:n % 4 * 128 + 128]

            def recurrence():
                pe.wait_ge(S["probs_ready"], seen.value("probs_ready"))
                turn_tokens(BI, [(0, X[0][:, 0, :]), (1, X[0][:, 1, :]), (2, X[1][:, 0, :])]).then_inc(S["nat_ready"], 1)
                pe.wait_ge(S["nat_copied"], seen.next("nat_copied"))
                pe.wait_ge(S["diag_in"], seen.next("diag_in"))
                q = proj[:, BQ:BQ + HB, :].rearrange("p h t -> p (h t)")
                for n in range(HB * NB):
                    mm = nc.tensor.matmul(block_out(n), k_sum[:, n * 128:n * 128 + 128], q[:, n * 128:n * 128 + 128],
                                          start=True, stop=True)
                mm.then_inc(S["lev_prod"], 1)
                pe.wait_ge(S["lev_taken"], seen.next("lev_taken"))
                for n in range(len(ITEMS)):
                    pe.wait_ge(S["lev_ready"], seen.next("lev_ready"))
                    if n >= 2:
                        pe.wait_ge(S["lev_taken"], seen.next("lev_taken"))
                    for j in range(6):
                        g = lev[n % 2][:, j * 128:j * 128 + 128]
                        mm = nc.tensor.matmul(X[n % 2][:, j // 4, j % 4 * 128:j % 4 * 128 + 128], g, g,
                                              start=True, stop=True)
                    mm.then_inc(S["lev_prod"], 1)
                seen.next("lev_taken", 2)
                pe.wait_ge(S["lev_taken"], seen.value("lev_taken"))
                for d in range(2):
                    pe.wait_ge(S["k_dec_ready"], seen.next("k_dec_ready"))
                    for n in range(8):
                        mm = nc.tensor.transpose(X[0][:, n // 4, n % 4 * 128:n % 4 * 128 + 128],
                                                 k_st[:, n // 2, n % 2 * 128:n % 2 * 128 + 128], ident)
                    mm.then_inc(S["kn_ready"], 1)
                    pe.wait_ge(S["kn_copied"], seen.next("kn_copied"))
                    if d == 1:
                        pe.wait_ge(S["st_taken"], seen.next("st_taken"))
                    for j in range(2):
                        for h in range(HB):
                            mm = nc.tensor.matmul(X[1][:, j, h * 128:h * 128 + 128], k_bn[d][0][:, h, j, :],
                                                  v_b[:, j * (1 + d), h, :], start=True, stop=True)
                    mm.then_inc(S["st_ready"], 1)
                pe.wait_ge(S["st_taken"], seen.next("st_taken"))
                pe.wait_ge(S["q_dec_ready"], seen.next("q_dec_ready"))
                pe.wait_ge(S["s_in_s"], seen.next("s_in_s", 32))
                for n in range(HB * NB):
                    h, b = n // NB, n % NB
                    ops = [(v_b[:, b, h, :], scores[:, n * 128:n * 128 + 128])]
                    if b:
                        ops += [((s_in if b == 1 + d else s_mid)[:, d, h, :],
                                 q_st[:, d, h, b * 128 - 128:b * 128]) for d in range(2)]
                    for j, (l_, r_) in enumerate(ops):
                        mm = nc.tensor.matmul(block_out(n), l_, r_, start=j == 0, stop=j == len(ops) - 1)
                mm.then_inc(S["o_ready"], 1)

            def mixer():
                pe.wait_ge(S["proj_ready"], seen.next("proj_ready", 19))
                turn_tokens(AV, [(0, X[0][:, 0, :]), (1, X[0][:, 1, :])]).then_inc(S["nat_ready"], 1)
                turn_tokens(AV, [(2, X[1][:, 0, :])])
                turn_tokens(AK, [(0, X[1][:, 1, :])]).then_inc(S["nat_ready"], 1)
                pe.wait_ge(S["ctx_in"], seen.next("ctx_in", 32))
                for h in range(HA):
                    mm = nc.tensor.transpose(S6[:, h * 128:h * 128 + 128], ctx_k[:, h * 128:h * 128 + 128], ident)
                mm.then_inc(S["nat_ready"], 1)
                pe.wait_ge(S["nat_copied"], seen.next("nat_copied"))
                swaps(AQ, 4, 0)
                pe.wait_ge(S["nat_copied"], seen.next("nat_copied"))
                swaps(AK, 4, 1)
                pe.wait_ge(S["nat_copied"], seen.next("nat_copied"))
                pe.wait_ge(S["rope_done"], seen.next("rope_done", 2))
                attention("a")
                head_sums()
                pe.wait_ge(S["o_root_ready"], seen.next("o_root_ready"))
                pe.wait_ge(S["c_sq_ready"], seen.next("c_sq_ready"))
                for t in range(5):
                    d = S5[:, 0:T] if t == 4 else X[t // 2][:, t % 2, 0:T]
                    mm = nc.tensor.matmul(d, head_ones, c_sq[:, t, :], start=True, stop=True)
                mm.then_inc(S["c_sum_ready"], 1)
                pe.wait_ge(S["c_norm_done"], seen.next("c_norm_done"))
                swaps(CQ, 4, 0)
                swaps(CK, 1, 1)
                for b in range(NB):
                    nc.tensor.transpose(S5[:, b * 128:b * 128 + 128], proj[:, CV, b * 128:b * 128 + 128], ident)
                nc.tensor.transpose(S5[:, 384:512], proj[:, CK, 0:SEQ], ident)
                pe.wait_ge(S["ctx_c_in"], seen.next("ctx_c_in", 32))
                nc.tensor.transpose(S6[:, 0:128], ctx_ck[:, :], ident).then_inc(S["nat_ready"], 1)
                pe.wait_ge(S["c_keys_ready"], seen.next("c_keys_ready"))
                for g in range(KVC):
                    mm = nc.tensor.matmul(X[1][:, g, :], con[:, C_DUP + g * 128:C_DUP + g * 128 + 128], c_kT[:, :],
                                          start=True, stop=True)
                mm.then_inc(S["dup_ready"], 1)
                pe.wait_ge(S["dup_copied"], seen.next("dup_copied"))
                pe.wait_ge(S["v_ready"], seen.next("v_ready"))
                seen.next("rope_done", 2)
                attention("c")
                recurrence()
                head_sums()
                seen.next("o_root_ready")

            for s in range(SLOTS):
                pe.sem_inc(unit_done[s], 1)
            pe.wait_ge(S["const_in"], 16)
            pe.wait_ge(S["rows_in"], 160)
            for l in range(DEPTH):
                nc.tensor.transpose(S5[:, l * V_ROWS:(l + 1) * V_ROWS], rows[0:V_ROWS, l, :], ident[0:V_ROWS, 0:V_ROWS])
            nc.tensor.transpose(S5[:, 2 * V_ROWS:2 * V_ROWS + M_ROWS], rows[0:M_ROWS, 2, :],
                                ident[0:M_ROWS, 0:M_ROWS]).then_inc(S["rows_turned"], 1)
            pe.wait_ge(S["x_in"], 32)
            for b in range(NB):
                if b == 2:
                    pe.wait_ge(S["x_copied"], 1)
                for k in range(KT):
                    mm = nc.tensor.transpose(X[b % 2][:, k // 4, k % 4 * 128:k % 4 * 128 + 128],
                                             x_rows[:, b, k * 128:k * 128 + 128], ident)
                mm.then_inc(S["x_turned"], 1)
            pe.wait_ge(S["c4_ready"], 1)
            loop("first", 4, first_units())
            with pe.Fori(0, DEPTH) as L:
                seen.enter("layer", L)
                for f in range(2):
                    loop(f"up{f}", 11, up_units(f), pre())
                    loop(f"down{f}", 2, down_units(f), ("act_ready", seen.next("act_ready", 11)))
                    y_sums()
                    if f == 0:
                        loop("proj", 4, proj_units(), pre())
                        stream(proj_tail_units())
                        mixer()
                        loop("merge", 4, merge_units(), ("split_ready", seen.next("split_ready", 3)))
                        loop("out", 2, out_units(), ("mg_ready", seen.next("mg_ready", 4)))
                        y_sums()
                seen.leave(DEPTH)
            pe.wait_ge(S["x_ready"], 4 + 12 * DEPTH)
            for b in range(NB):
                if b == 2:
                    pe.wait_ge(S["y_out_ready"], 1)
                for k in range(KT):
                    mm = nc.tensor.transpose(X[b % 2][:, k // 4, k % 4 * 128:k % 4 * 128 + 128],
                                             x[:, k, b * 128:b * 128 + 128], ident)
                mm.then_inc(S["y_turned"], 1)

        @block.scalar
        def _(act):
            seen = Seen(turns.setdefault("ACT", {}), learn)
            for s in range(SLOTS):
                seen.start(("done", s), 1)
            A = nc.scalar.activation

            def stream(units, outputs=None, lag=3):
                done = [seen.next(("done", u.slot)) for u in units]
                pending = [(j, u) for j, u in enumerate(units) if u.last and outputs and u.tag in outputs]
                for j, u in enumerate(units):
                    act.wait_ge(loaded[u.slot], seen.next(("in", u.slot), 16))
                    act.wait_ge(unit_done[u.slot], seen.next(("reuse", u.slot)))
                    A(slot(w_hi, u), slot(raw, u), ACT.Copy).then_inc(hi_ready[u.slot], 1)
                    while pending and (pending[0][0] + lag <= j or j == len(units) - 1):
                        k, v = pending.pop(0)
                        act.wait_ge(unit_done[v.slot], done[k])
                        outputs[v.tag](v)

            def loop(name, count, units, outputs=None):
                with act.Fori(0, count) as i:
                    seen.enter(name, i)
                    stream(units, outputs)
                    seen.leave(count)

            def round_unit(u):
                act.wait_ge(loaded[u.slot], seen.next(("in", u.slot), 16))
                act.wait_ge(unit_done[u.slot], seen.next(("reuse", u.slot)))
                A(slot(w_hi, u), slot(raw, u), ACT.Copy).then_inc(hi_ready[u.slot], 1)

            def prefill(units):
                for u in units[:SLOTS]:
                    round_unit(u)

            def turn_ahead(units, outputs, last):
                done = [seen.next(("done", u.slot)) for u in units]
                for j, u in enumerate(units):
                    if u.last and u.tag in outputs:
                        act.wait_ge(unit_done[u.slot], done[j])
                        outputs[u.tag](u)
                    if j + SLOTS < len(units) or not last:
                        round_unit(units[(j + SLOTS) % len(units)])

            def loop_ahead(name, count, units, outputs):
                with act.Fori(0, count - 1) as i:
                    seen.enter(name, i)
                    turn_ahead(units, outputs, False)
                    seen.leave(count - 1)
                turn_ahead(units, outputs, True)

            def inverse_root(parts, scale, dst, src):
                for out_, sums in parts:
                    ins = A(out_, sums, ACT.Ln, bias=eps[:, 0:1], scale=scale)
                ins.then_inc(S["act_step"], 1)
                act.wait_ge(S["act_step"], seen.next("act_step"))
                return A(dst, src, ACT.Exp, scale=-0.5)

            def root_of_sums():
                act.wait_ge(S["sum_ready"], seen.next("sum_ready"))
                A(root[:, :], S5[:, 0:T], ACT.Sqrt, bias=eps[:, 0:1], scale=1.0 / D).then_inc(S["root_ready"], 1)

            def pre():
                for c in range(4):
                    act.wait_ge(S["x_ready"], seen.next("x_ready"))
                    A(sq[:, 2 * c:2 * c + 2, :], x[:, 2 * c:2 * c + 2, :], ACT.Square).then_inc(S["x_sq_ready"], 1)
                root_of_sums()
                for c in range(4):
                    act.wait_ge(S["norm_ready"], seen.next("norm_ready"))
                    A(h_hi[:, 2 * c:2 * c + 2, :], sq[:, 2 * c:2 * c + 2, :], ACT.Copy).then_inc(S["hh_ready"], 1)

            def gate_silu(u):
                act.wait_ge(S["act_ready"], seen.next("act_ready"))
                A(silu[:, :, :], X[0][:, :, 0:T], ACT.Silu).then_inc(x_free[0], 1)

            def head_roots():
                act.wait_ge(S["o_sum_ready"], seen.next("o_sum_ready"))
                inverse_root([(o_rt[:, 0:2, :], X[0][:, :, 0:T]), (o_rt[:, 2:4, :], X[1][:, :, 0:T])], 1.0 / 128,
                             o_rt[:, :, :], o_rt[:, :, :]).then_inc(S["o_root_ready"], 1)

            def attention(kind):
                def exps(n):
                    w = SEQ if STEPS[n][1] == 0 else PAST + LAT
                    act.wait_ge(S["max_ready"], seen.next("max_ready"))
                    for c in range(2):
                        e = A(p[n % 2][:, c, 0:w], X[n % 2][:, c, 0:w], ACT.Exp, bias=nmax[:, n % 2, c:c + 1],
                              accum_out=esum[:, n % 2, c:c + 1])
                    e.then_inc(S["probs_ready"], 1)

                def copy(n):
                    w = SEQ if STEPS[n][1] == 0 else PAST + LAT
                    act.wait_ge(S["turned_ready"], seen.next("turned_ready"))
                    if n >= 1:
                        act.wait_ge(S["out_ready"], seen.next("out_ready"))
                    A(pT[:, 0, 0:w], S5[:, 0:w], ACT.Copy) if kind == "c" else \
                        A(pT[:, 0, 0:w], S5[:, 0:w], ACT.Copy).then_inc(S["turned_copied"], 1)
                    if kind == "c":
                        A(pT[:, 1, 0:w], S6[:, 0:w], ACT.Copy).then_inc(S["turned_copied"], 1)

                exps(0)
                for n in range(len(STEPS)):
                    if n + 1 < len(STEPS):
                        exps(n + 1)
                    copy(n)
                seen.next("out_ready")

            def mixer_loads(L):
                act.dma_start(ctx_k[:, :], io["cache_a_k"][ds(L, 1)].rearrange("l t c -> t (l c)")).then_inc(S["ctx_in"], 16)
                act.dma_start(ctx_v[:, :], io["cache_a_v"][ds(L, 1)].rearrange("l t c -> t (l c)")).then_inc(S["ctx_in"], 16)

            def mixer(L):
                act.wait_ge(S["nat_copied"], seen.next("nat_copied", 2))
                act.dma_start(out["new_a_v"][ds(L, 1)].rearrange("l t c -> t (l c)"), v_nat[:, 0, :]).then_inc(S["stored_a"], 16)
                act.dma_start(out["new_a_k"][ds(L, 1)].rearrange("l t c -> t (l c)"), k_nat[:, :]).then_inc(S["stored_a"], 16)
                seen.next("nat_copied")
                A(proj[:, BQ:BQ + 4, :], proj[:, BQ:BQ + 4, :], ACT.Silu)
                A(proj[:, BG:BG + 4, :], proj[:, BG:BG + 4, :], ACT.Silu).then_inc(S["bg_ready"], 1)
                prefill(merge_units())
                attention("a")
                act.wait_ge(S["out_taken"], seen.next("out_taken", len(STEPS)))
                A(o_sq[:, :, :], proj[:, AQ:AQ + 4, :], ACT.Square).then_inc(S["o_sq_ready"], 1)
                head_roots()
                act.wait_ge(S["stored_a"], seen.next("stored_a", 32))
                act.wait_ge(S["br_ready"], seen.next("br_ready"))
                act.dma_start(ctx_ck[:, :], io["cache_c_k"][ds(L, 1)].rearrange("l t c -> t (l c)")).then_inc(S["ctx_c_in"], 16)
                act.dma_start(ctx_cv[:, :], io["cache_c_v"][ds(L, 1)].rearrange("l t c -> t (l c)")).then_inc(S["ctx_c_in"], 16)
                A(c_sq[:, :, :], proj[:, CQ:CQ + 5, :], ACT.Square).then_inc(S["c_sq_ready"], 1)
                act.wait_ge(S["c_sum_ready"], seen.next("c_sum_ready"))
                inverse_root([(c_rt[:, 0:2, :], X[0][:, :, 0:T]), (c_rt[:, 2:4, :], X[1][:, :, 0:T]),
                              (c_rt[:, 4, :], S5[:, 0:T])], 1.0 / 64, c_rt[:, :, :], c_rt[:, :, :]) \
                    .then_inc(S["c_root_ready"], 1)
                act.wait_ge(S["dup_ready"], seen.next("dup_ready"))
                A(c_kd[:, :, :], X[1][:, :, :], ACT.Copy).then_inc(S["dup_copied"], 1)
                act.wait_ge(S["v_ready"], seen.next("v_ready"))
                act.dma_start(out["new_c_v"][ds(L, 1)].rearrange("l t c -> t (l c)"), c_nat[:, 0:128]).then_inc(S["stored_c"], 16)
                act.dma_start(out["new_c_k"][ds(L, 1)].rearrange("l t c -> t (l c)"), c_nat[:, 384:512]).then_inc(S["stored_c"], 16)
                attention("c")
                seen.next("nat_copied")
                act.wait_ge(S["out_taken"], seen.next("out_taken", len(STEPS)))
                act.wait_ge(S["stored_c"], seen.next("stored_c", 32))
                for d in range(2):
                    act.dma_start(s_in[:, d, :, :], io["state_hgrn"][ds(L, 1), d].rearrange("l h k v -> k (l h) v")) \
                        .then_inc(S["s_in_s"], 16)
                for d, z in enumerate((BFF, BFB)):
                    zz = proj[:, z:z + 4, :].rearrange("p h t -> p (h t)")
                    A((b_f, b_b)[d][:, :], zz, ACT.Sigmoid)
                    A(zz, zz, ACT.Sigmoid, scale=-1.0).then_inc(S["rec_gate_ready"], 1)
                for d in range(2):
                    act.wait_ge(S["f_ready"], seen.next("f_ready"))
                    A((b_f, b_b)[d][:, :], (b_f, b_b)[d][:, :], ACT.Ln).then_inc(S["logf_ready"], 1)
                for n in range(len(ITEMS)):
                    act.wait_ge(S["dec_ready"], seen.next("dec_ready"))
                    A(dec[n % 2][:, :], dec[n % 2][:, :], ACT.Exp).then_inc(S["exp_ready"], 1)
                act.wait_ge(S["st_exp"], seen.next("st_exp"))
                bf4 = b_f[:, :].rearrange("p (h t) -> p h t", t=T)
                bb5 = b_b[:, :].rearrange("p (h b t) -> p h b t", h=HB, b=NB)
                A(q_st[:, 0, :, :], bf4[:, :, SEQ:T], ACT.Exp)
                A(q_st[:, 1, :, :], q_st[:, 1, :, :], ACT.Exp)
                for d in range(2):
                    A(dend[:, d, :], ends[:, d, 1 + d::NB], ACT.Exp)
                A(k_st[:, :, :], k_st[:, :, :], ACT.Exp).then_inc(S["exp_ready"], 1)
                act.wait_ge(S["kn_ready"], seen.next("kn_ready"))
                A(k_st[:, :, :].rearrange("p h (b t) -> p h b t", b=2), bb5[:, :, 0:3:2, :], ACT.Exp) \
                    .then_inc(S["exp_ready"], 1)
                seen.next("kn_ready")
                for d in range(2):
                    act.wait_ge(S["st_taken"], seen.next("st_taken"))
                    act.dma_start(out["new_hgrn"][ds(L, 1), d].rearrange("l h k v -> k (l h) v"), k_bn[d][1][:, :, :]) \
                        .then_inc(S["stored_s"], 16)
                act.wait_ge(S["o_taken"], seen.next("o_taken"))
                A(o_sq[:, :, :], proj[:, BQ:BQ + 4, :], ACT.Square).then_inc(S["o_sq_ready"], 1)
                head_roots()
                act.wait_ge(S["br_ready"], seen.next("br_ready"))
                act.wait_ge(S["stored_s"], seen.next("stored_s", 32))
                for b, t0 in enumerate((AQ, BQ, CQ)):
                    A(br_hi[:, 4 * b:4 * b + 4, :], proj[:, t0:t0 + 4, :], ACT.Copy).then_inc(S["br_hi_ready"], 1)
                act.wait_ge(S["split_ready"], seen.next("split_ready", 3))

            def sigmoid(b):
                def go(u):
                    if b == 0:
                        act.wait_ge(S["mg_ready"], seen.next("mg_ready"))
                    A(gate[b][:, :, :], X[u.dest][:, :, 0:T], ACT.Sigmoid).then_inc(x_free[u.dest], 1)
                return go

            act.wait_ge(S["vec_ready"], 1)
            A(c_act[:, :, :].rearrange("p k g -> p g k"), misc[:, 0:16].rearrange("p (g k) -> p g k", g=2), ACT.Silu) \
                .then_inc(S["act_step"], 1)
            act.wait_ge(S["act_step"], seen.next("act_step"))
            A(c4[:, :, 0:2], c_act[:, :, :], ACT.Copy).then_inc(S["c_ready"], 1)
            A(lb[:, 1, :, :], lb_d[:, :, :], ACT.Sigmoid)
            A(omlb[:, 1, :, :], lb_d[:, :, :], ACT.Sigmoid, scale=-1.0)
            A(lam_s[:, :, :], lam_s[:, :, :], ACT.Exp).then_inc(S["c_ready"], 1)
            loop("first", 4, first_units())
            with act.Fori(0, DEPTH) as L:
                seen.enter("layer", L)
                for f in range(2):
                    prefill(up_units(f))
                    pre()
                    loop_ahead(f"up{f}", 11, up_units(f), {"gate": gate_silu})
                    loop(f"down{f}", 2, down_units(f))
                    root_of_sums()
                    if f == 0:
                        prefill(proj_units())
                        pre()
                        mixer_loads(L)
                        loop_ahead("proj", 4, proj_units(), {})
                        stream(proj_tail_units())
                        mixer(L)
                        loop_ahead("merge", 4, merge_units(), {("g", b): sigmoid(b) for b in range(3)})
                        loop("out", 2, out_units())
                        root_of_sums()
                seen.leave(DEPTH)
            act.wait_ge(S["y_out_ready"], 1)
            act.dma_start(out["y_prompt"], x_rows[:, 0, :]).then_inc(S["stored_y"], 16)
            for b in (1, 2):
                act.wait_ge(S["y_out_ready"], b + 1)
                act.dma_start(out["y_sample"][b * 128 - 128:b * 128, :], x_rows[:, b, :]).then_inc(S["stored_y"], 16)
            act.wait_ge(S["stored_y"], 48)

        @block.vector
        def _(dve):
            seen = Seen(turns.setdefault("DVE", {}), learn)
            V = nc.vector
            for s in range(SLOTS):
                seen.start(("done", s), 1)
            for d in range(2):
                seen.start(("mine", d), 1)
            seen.start("my_ada", 1)

            def step(ins):
                ins.then_inc(S["dve_step"], 1)
                dve.wait_ge(S["dve_step"], seen.next("dve_step"))

            def wide(v, n):
                return v.unsqueeze(1).broadcast_to([128, n, v.shape[-1]])

            def stream(units, outputs, i, lag=3):
                done = [seen.next(("done", u.slot)) for u in units]
                key = lambda u: u.tag if u.tag in outputs else u.tag[0]
                pending = [(j, u) for j, u in enumerate(units) if u.last and key(u) in outputs]
                for j, u in enumerate(units):
                    there = seen.next(("hi", u.slot))
                    if u.split == "dve":
                        dve.wait_ge(hi_ready[u.slot], there)
                        V.tensor_tensor(slot(w_lo, u), slot(raw, u), slot(w_hi, u), SUB).then_inc(lo_ready[u.slot], 1)
                    while pending and (pending[0][0] + lag <= j or j == len(units) - 1):
                        k, v = pending.pop(0)
                        dve.wait_ge(unit_done[v.slot], done[k])
                        outputs[key(v)](v, i)

            def loop(name, count, units, outputs, lag=3):
                with dve.Fori(0, count) as i:
                    seen.enter(name, i)
                    stream(units, outputs, i, lag)
                    seen.leave(count)

            def ada_out(u, i):
                _, first, per = u.tag
                V.tensor_reduce(mod_t[:, :, :], Ab[:, 0:8].rearrange("p (m h g) -> p m g h", m=2, h=2), AX.X, ADD) \
                    .then_inc(ada_free, 1)
                dve.wait_ge(ada_free, seen.next("my_ada"))
                step(V.tensor_scalar(mod[:, ds(i * (2 * per) + 2 * first, 2), :], mod_t[:, :, :], 1.0, None, MUL))

            def layer_vec(L, r0):
                return vec[:, ds(L, 1), r0:r0 + KT, :].rearrange("p l k g -> p (l k) g")

            def pre_factors(L, n):
                m0 = (MOD_TILES, 3 * KT, 6 * KT)[n]
                sh, sc = mod[:, m0:m0 + KT, :], mod[:, m0 + KT:m0 + 2 * KT, :]
                V.tensor_tensor(mB[:, :, :], sh, layer_vec(L, 3 * n * KT), ADD)
                step(V.tensor_tensor(mA[:, :, :], sc, layer_vec(L, (3 * n + 1) * KT), ADD))
                step(V.tensor_scalar(mA[:, :, :], mA[:, :, :], 1.0, None, ADD))
                step(V.tensor_tensor(mA[:, :, :], mA[:, :, :], layer_vec(L, V_PRE + n * KT), MUL))

            def marked(ins):
                ins.then_inc(S["dve_step"], 1)
                return seen.next("dve_step")

            GROUPS = list(enumerate(((0, SEQ), (SEQ, T))))

            def pre():
                dve.wait_ge(S["root_ready"], seen.next("root_ready"))
                step(V.reciprocal(rinv[:, :], root[:, :]))
                made = {}

                def scale(c):
                    t = slice(2 * c, 2 * c + 2)
                    made[c] = marked(V.tensor_tensor(sq[:, t, :], x[:, t, :], wide(rinv[:, :], 2), MUL))

                def modulate(c):
                    dve.wait_ge(S["dve_step"], made[c])
                    for k in (2 * c, 2 * c + 1):
                        for g, (t0, t1) in GROUPS:
                            ins = V.tensor_scalar(sq[:, k, t0:t1], sq[:, k, t0:t1], mA[:, k, g:g + 1],
                                                  mB[:, k, g:g + 1], MUL, ADD)
                    ins.then_inc(S["norm_ready"], 1)

                for c in range(5):
                    if c < 4:
                        scale(c)
                    if c >= 1:
                        modulate(c - 1)
                V.memset(y_sum[:, :], 0.0).then_inc(S["dve_step"], 1)
                seen.next("dve_step")

            def post_factors(L, n):
                m0 = (3 * n + 2) * KT
                step(V.tensor_tensor(mG[:, :, :], mod[:, m0:m0 + KT, :], layer_vec(L, m0), ADD))
                step(V.tensor_tensor(mG[:, :, :], mG[:, :, :], layer_vec(L, V_POST + n * KT), MUL))
                if n != 1:
                    step(V.tensor_scalar(mG[:, :, :], mG[:, :, :], 0.5, None, MUL))

            def post():
                dve.wait_ge(S["root_ready"], seen.next("root_ready"))
                step(V.reciprocal(rinv[:, :], root[:, :]))
                made = {}
                for c in range(5):
                    if c < 4:
                        t = slice(2 * c, 2 * c + 2)
                        made[c] = marked(V.tensor_tensor(y[:, t, :], y[:, t, :], wide(rinv[:, :], 2), MUL))
                    if c >= 1:
                        dve.wait_ge(S["dve_step"], made[c - 1])
                        for k in (2 * c - 2, 2 * c - 1):
                            for g, (t0, t1) in GROUPS:
                                ins = V.scalar_tensor_tensor(x[:, k, t0:t1], y[:, k, t0:t1], mG[:, k, g:g + 1],
                                                             x[:, k, t0:t1], MUL, ADD)
                        ins.then_inc(S["x_ready"], 1)

            def up_out(u, i):
                dve.wait_ge(x_free[0], seen.next(("mine", 0)))
                V.tensor_tensor(prod[:, :, :], X[1][:, :, 0:T], silu[:, :, :], MUL).then_inc(x_free[1], 1)
                dve.wait_ge(x_free[1], seen.next(("mine", 1)))
                step(V.tensor_scalar(act_hi[:, ds(i * 2, 2), :], prod[:, :, :], 1.0, None, MUL))
                V.tensor_tensor(act_lo[:, ds(i * 2, 2), :], prod[:, :, :], act_hi[:, ds(i * 2, 2), :], SUB) \
                    .then_inc(S["act_ready"], 1)

            def y_out(t):
                def go(u, i):
                    yy = y[:, ds(t(i), 2), :]
                    V.tensor_scalar(yy, X[u.dest][:, :, 0:T], 1.0, None, MUL).then_inc(x_free[u.dest], 1)
                    dve.wait_ge(x_free[u.dest], seen.next(("mine", u.dest)))
                    step(V.tensor_tensor(prod[:, :, :], yy, yy, MUL))
                    step(V.tensor_tensor(y_sum[:, :], y_sum[:, :], prod[:, 0, :], ADD))
                    V.tensor_tensor(y_sum[:, :], y_sum[:, :], prod[:, 1, :], ADD).then_inc(S["y_sq_ready"], 1)
                    dve.wait_ge(S["y_sq_ready"], seen.next("my_sum"))
                return go

            def proj_out(t):
                def go(u, i):
                    V.tensor_scalar(proj[:, ds(t(i), 2), :], X[u.dest][:, :, 0:T], 1.0, None, MUL) \
                        .then_inc(x_free[u.dest], 1)
                    dve.wait_ge(x_free[u.dest], seen.next(("mine", u.dest)))
                    dve.sem_inc(S["proj_ready"], 1)
                return go

            def tail_out(j):
                def go(u, i):
                    V.tensor_copy(proj[:, 32 + 2 * j:34 + 2 * j, :], X[u.dest][:, :, 0:T]).then_inc(x_free[u.dest], 1)
                    dve.wait_ge(x_free[u.dest], seen.next(("mine", u.dest)))
                    dve.sem_inc(S["proj_ready"], 1)
                return go

            def rope(tile0, tiles, xb):
                if tiles > 1:
                    s = X[xb][:, :, :].rearrange("p a (b c) -> p (a b) c", b=2)
                    tt, uu = rope_t[:, :, :], rope_u[:, :, :]
                else:
                    s, tt, uu = X[xb][:, 0:1, 0:LAT], rope_t[:, 0:1, :], rope_u[:, 0:1, :]
                v = proj[:, tile0:tile0 + tiles, SEQ:T]
                dve.wait_ge(S["swap_ready"], seen.next("swap_ready"))
                V.tensor_tensor(tt, s, wide(con[:, C_SIN:C_SIN + LAT], tiles), MUL)
                step(V.tensor_tensor(uu, v, wide(con[:, C_COS:C_COS + LAT], tiles), MUL))
                V.tensor_tensor(v, tt, uu, ADD).then_inc(S["rope_done"], 1)
                dve.wait_ge(S["rope_done"], seen.next("my_rope"))

            def attention(kind):
                def maxima(n):
                    w = SEQ if STEPS[n][1] == 0 else PAST + LAT
                    dve.wait_ge(S["scores_ready"], seen.next("scores_ready"))
                    V.tensor_reduce(nmax[:, n % 2, :], X[n % 2][:, :, 0:w], AX.X, ALU.max, negate=True) \
                        .then_inc(S["max_ready"], 1)

                def weights(n):
                    w = SEQ if STEPS[n][1] == 0 else PAST + LAT
                    dve.wait_ge(S["probs_ready"], seen.next("probs_ready"))
                    step(V.reciprocal(rsum[:, :], esum[:, n % 2, :]))
                    if kind == "a":
                        V.tensor_scalar(comb[:, 0:w], p[n % 2][:, 0, 0:w], rsum[:, 0:1], None, MUL)
                        step(V.tensor_tensor(rsum[:, 1:2], rsum[:, 1:2], one_l[:, 0:1], MUL))
                        V.scalar_tensor_tensor(comb[:, 0:w], p[n % 2][:, 1, 0:w], rsum[:, 1:2], comb[:, 0:w], MUL, ADD) \
                            .then_inc(S["comb_ready"], 1)
                    else:
                        V.tensor_scalar(p[n % 2][:, 0, 0:w], p[n % 2][:, 0, 0:w], rsum[:, 0:1], None, MUL)
                        V.tensor_scalar(p[n % 2][:, 1, 0:w], p[n % 2][:, 1, 0:w], rsum[:, 1:2], None, MUL) \
                            .then_inc(S["comb_ready"], 1)
                    dve.wait_ge(S["comb_ready"], seen.next("my_comb"))

                def take(n):
                    h, b = STEPS[n]
                    t = slice(b * 128, b * 128 + 128)
                    dve.wait_ge(S["out_ready"], seen.next("out_ready"))
                    if kind == "a":
                        V.tensor_copy(proj[:, AQ + h, t], S7[:, 0:128]).then_inc(S["out_taken"], 1)
                    else:
                        V.tensor_copy(proj[0:64, CQ + h, t], S7[0:64, 0:128])
                        V.tensor_copy(proj[64:128, CQ + h, t], S7[64:128, 128:256]).then_inc(S["out_taken"], 1)

                maxima(0)
                for n in range(len(STEPS) + 1):
                    if n + 1 < len(STEPS):
                        maxima(n + 1)
                    if n < len(STEPS):
                        weights(n)
                    if n >= 1:
                        take(n - 1)

            def flat(tile0):
                return proj[:, tile0:tile0 + 4, :].rearrange("p h t -> p (h t)")

            def norm_heads(tile0, g):
                dve.wait_ge(S["o_root_ready"], seen.next("o_root_ready"))
                return V.scalar_tensor_tensor(flat(tile0), flat(tile0), g, o_rt[:, :, :].rearrange("p h t -> p (h t)"),
                                              MUL, MUL)

            def recurrence():
                dve.wait_ge(S["nat_ready"], seen.next("nat_ready"))
                V.tensor_copy(v_b[:, 0:2, :, :].rearrange("p b h c -> p b (h c)"), X[0][:, :, :])
                V.tensor_copy(v_b[:, 2, :, :].rearrange("p h c -> p (h c)"), X[1][:, 0, :]).then_inc(S["nat_copied"], 1)
                for d, z in enumerate((BFF, BFB)):
                    dve.wait_ge(S["rec_gate_ready"], seen.next("rec_gate_ready"))
                    bd = (b_f, b_b)[d]
                    for h in range(HB):
                        V.tensor_scalar(bd[:, h * T:h * T + T], bd[:, h * T:h * T + T], lbl[:, 1, d, h:h + 1],
                                        lbl[:, 0, d, h:h + 1], MUL, ADD)
                        ins = V.tensor_scalar(proj[:, z + h, :], proj[:, z + h, :], lbl[:, 1, d, h:h + 1], None, MUL)
                    step(ins)
                    V.tensor_scalar(bd[:, :], bd[:, :], 2.0 ** -64, None, ALU.max).then_inc(S["f_ready"], 1)
                dve.wait_ge(S["logf_ready"], seen.next("logf_ready"))
                step(V.tensor_tensor_scan(b_f[:, :], reset[:, :], b_f[:, :], 0.0, MUL, ADD))
                dve.wait_ge(S["logf_ready"], seen.next("logf_ready"))
                step(V.tensor_tensor_scan(scores[:, :], reset[:, :], b_b[:, :], 0.0, MUL, ADD))
                V.tensor_copy(ends[:, 0, :], b_f[:, 127::128])
                V.tensor_copy(ends[:, 1, :], scores[:, 127::128])
                step(V.tensor_tensor(b_b[:, :], scores[:, :], b_b[:, :], SUB))
                dve.wait_ge(S["bg_ready"], seen.next("bg_ready"))
                V.tensor_tensor(k_sum[:, :], flat(BFF), flat(BFB), ADD).then_inc(S["diag_in"], 1)
                dve.wait_ge(S["lev_prod"], seen.next("lev_prod"))
                blocks = scores[:, :].rearrange("p (n c) -> p n c", c=128)
                V.tensor_tensor(blocks[:, 0:8, :], X[0][:, :, :].rearrange("p a (b c) -> p (a b) c", c=128),
                                wide(ident, 8), MUL)
                step(V.tensor_tensor(blocks[:, 8:12, :], X[1][:, 0, :].rearrange("p (b c) -> p b c", c=128),
                                     wide(ident, 4), MUL))
                dve.sem_inc(S["lev_taken"], 1)

                def products(n):
                    d, l, half = ITEMS[n]
                    par, b = LEVELS[l], LEVELS[l] // 2
                    e, g, q, k = (t.rearrange("p (n c) -> p n c", c=par) for t in (
                        dec[n % 2][:, :], lev[n % 2][:, :], flat(BQ)[:, half * 768:half * 768 + 768],
                        flat((BFF, BFB)[d])[:, half * 768:half * 768 + 768]))
                    first, second = (k, q) if d == 0 else (q, k)
                    dve.wait_ge(S["exp_ready"], seen.next("exp_ready"))
                    V.tensor_tensor(g[:, :, 0:b], e[:, :, 0:b], first[:, :, 0:b], MUL)
                    V.tensor_tensor(g[:, :, b:], e[:, :, b:], second[:, :, b:], MUL).then_inc(S["lev_ready"], 1)

                def pick(n):
                    d, l, half = ITEMS[n]
                    dve.wait_ge(S["lev_taken"], seen.next("my_lev"))
                    dve.wait_ge(S["lev_prod"], seen.next("lev_prod"))
                    V.memset(tick[:, :], 0.0)
                    for a, nb in ((0, 4), (1, 2)):
                        m = wide(masks[:, d, l, :], nb)
                        ins = V.copy_predicated(blocks[:, half * 6 + 4 * a:half * 6 + 4 * a + nb, :], m,
                                                X[n % 2][:, a, 0:nb * 128].rearrange("p (b c) -> p b c", c=128))
                    ins.then_inc(S["lev_taken"], 1)

                for n in range(len(ITEMS) + 1):
                    if n < len(ITEMS):
                        products(n)
                    if n >= 1:
                        pick(n - 1)
                dve.wait_ge(S["lev_taken"], seen.next("my_lev"))
                e4 = ends[:, :, :].rearrange("p d (h b) -> p d h b", b=NB)
                bb4 = b_b[:, :].rearrange("p (h b t) -> p h b t", h=HB, b=NB)
                bf4 = b_f[:, :].rearrange("p (h b t) -> p h b t", h=HB, b=NB)
                qs4 = q_st[:, 1, :, :].rearrange("p h (b t) -> p h b t", b=2)
                ks4 = k_st[:, :, :].rearrange("p h (b t) -> p h b t", b=2)
                for h in range(HB):
                    V.tensor_tensor(qs4[:, h], e4[:, 1, h, 1:3].unsqueeze(2).broadcast_to([128, 2, 128]), bb4[:, h, 1:3, :], SUB)
                    ins = V.tensor_tensor(ks4[:, h], e4[:, 0, h, 0:2].unsqueeze(2).broadcast_to([128, 2, 128]), bf4[:, h, 0:2, :], SUB)
                ins.then_inc(S["st_exp"], 1)
                dve.wait_ge(S["exp_ready"], seen.next("exp_ready"))
                q3 = proj[:, BQ:BQ + 4, SEQ:T]
                V.tensor_tensor(k_st[:, :, :], k_st[:, :, :], proj[:, BFF:BFF + 4, 0:256], MUL).then_inc(S["k_dec_ready"], 1)
                for d in range(2):
                    ins = V.tensor_tensor(q_st[:, d, :, :], q_st[:, d, :, :], q3, MUL)
                ins.then_inc(S["q_dec_ready"], 1)
                for d in range(2):
                    dve.wait_ge(S["kn_ready"], seen.next("kn_ready"))
                    V.tensor_copy(k_bn[d][0][:, :, :, :].rearrange("p (a h) b c -> p a (h b c)", a=2), X[0][:, :, :]) \
                        .then_inc(S["kn_copied"], 1)
                    if d == 0:
                        dve.wait_ge(S["exp_ready"], seen.next("exp_ready"))
                        pb4 = proj[:, BFB:BFB + 4, :].rearrange("p h (b t) -> p h b t", b=NB)
                        for h in range(HB):
                            ins = V.tensor_tensor(ks4[:, h], ks4[:, h], pb4[:, h, 0:3:2, :], MUL)
                        ins.then_inc(S["k_dec_ready"], 1)
                    dve.wait_ge(S["st_ready"], seen.next("st_ready"))
                    if d == 0:
                        dve.wait_ge(S["s_in_s"], seen.next("s_in_s", 32))
                    for h in range(HB):
                        V.scalar_tensor_tensor(s_mid[:, d, h, :], s_in[:, d, h, :], dend[:, d, h:h + 1],
                                               X[1][:, 1, h * 128:h * 128 + 128], MUL, ADD)
                    V.tensor_copy(k_bn[d][1][:, :, :].rearrange("p h c -> p (h c)"), X[1][:, 0, :]).then_inc(S["st_taken"], 1)
                dve.wait_ge(S["o_ready"], seen.next("o_ready"))
                o3 = flat(BQ)
                V.tensor_scalar(o3[:, 0:1024].rearrange("p (a c) -> p a c", a=2), X[0][:, :, :], 128 ** -0.5, None, MUL)
                V.tensor_scalar(o3[:, 1024:1536], X[1][:, 0, :], 128 ** -0.5, None, MUL).then_inc(S["o_taken"], 1)
                step(norm_heads(BQ, one_l[:, 2:3]))
                V.tensor_tensor(flat(BQ), flat(BQ), flat(BG), MUL).then_inc(S["br_ready"], 1)

            def layer_factors(L):
                for j, src in enumerate((neg_lam[:, ds(L, 1)], sub_g[:, ds(L, 1)], misc[:, ds(L + M_GN, 1)],
                                         qn_g[:, ds(L, 1)], misc[:, ds(L + M_KN, 1)])):
                    V.tensor_scalar(one_l[:, j:j + 1], src, 1.0, None, MUL)
                V.tensor_scalar(lbl[:, 0, :, :], lb[:, ds(L, 1)].rearrange("p l d h -> p (l d) h"), 1.0, None, MUL)
                step(V.tensor_scalar(lbl[:, 1, :, :], omlb[:, ds(L, 1)].rearrange("p l d h -> p (l d) h"), 1.0, None, MUL))

            def mixer(L):
                layer_factors(L)
                dve.wait_ge(S["nat_ready"], seen.next("nat_ready"))
                V.tensor_copy(v_nat[:, 0:2, :], X[0][:, :, :]).then_inc(S["nat_copied"], 1)
                dve.wait_ge(S["nat_ready"], seen.next("nat_ready"))
                V.tensor_copy(v_nat[:, 2, :], X[1][:, 0, :])
                V.tensor_copy(k_nat[:, :], X[1][:, 1, :]).then_inc(S["nat_copied"], 1)
                dve.wait_ge(S["nat_ready"], seen.next("nat_ready"))
                V.tensor_copy(ctx_kT[:, :, :].rearrange("p h c -> p (h c)"), S6[:, :]).then_inc(S["nat_copied"], 1)
                rope(AQ, 4, 0)
                step(V.tensor_scalar(flat(AQ), flat(AQ), 64 ** -0.5, None, MUL))
                rope(AK, 4, 1)
                attention("a")
                norm_heads(AQ, one_l[:, 1:2]).then_inc(S["br_ready"], 1)
                dve.wait_ge(S["c_root_ready"], seen.next("c_root_ready"))
                V.scalar_tensor_tensor(flat(CQ), flat(CQ), one_l[:, 3:4], c_rt[:, 0:4, :].rearrange("p h t -> p (h t)"),
                                       MUL, MUL)
                step(V.scalar_tensor_tensor(proj[:, CK, :], proj[:, CK, :], one_l[:, 4:5], c_rt[:, 4, :], MUL, MUL))
                dve.sem_inc(S["c_norm_done"], 1)
                rope(CQ, 4, 0)
                rope(CK, 1, 1)
                dve.wait_ge(S["nat_ready"], seen.next("nat_ready"))
                V.tensor_copy(c_kT[:, 0:PAST], S6[:, 0:128])
                V.tensor_copy(c_kT[:, PAST:], proj[:, CK, :]).then_inc(S["c_keys_ready"], 1)
                step(V.tensor_copy(c_nat[:, :], S5[:, :]))
                for g in range(KVC):
                    V.tensor_copy(c_vd[:, g, 0:3, :, :],
                                  c_nat[:, 0:384].rearrange("p (b c) -> p b c", b=3)[:, :, g * 64:g * 64 + 64]
                                  .unsqueeze(2).broadcast_to([128, 3, 2, 64]))
                    if g == 0:
                        dve.wait_ge(S["ctx_c_in"], seen.next("ctx_c_in", 32))
                    ins = V.tensor_copy(c_vd[:, g, 3, :, :], wide(ctx_cv[:, g * 64:g * 64 + 64], 2))
                ins.then_inc(S["v_ready"], 1)
                attention("c")
                recurrence()
                for b, t0 in enumerate((AQ, BQ, CQ)):
                    dve.wait_ge(S["br_hi_ready"], seen.next("br_hi_ready"))
                    V.tensor_tensor(br_lo[:, 4 * b:4 * b + 4, :], proj[:, t0:t0 + 4, :], br_hi[:, 4 * b:4 * b + 4, :], SUB) \
                        .then_inc(S["split_ready"], 1)

            def merge_out(b):
                def go(u, i):
                    dst = acc if b == 0 else acc2
                    if b == 0:
                        dve.wait_ge(x_free[0], seen.next(("mine", 0), 2))
                        dve.wait_ge(x_free[1], seen.next(("mine", 1)))
                    V.tensor_tensor(dst[:, :, :], X[u.dest][:, :, 0:T], gate[b][:, :, :], MUL).then_inc(x_free[u.dest], 1)
                    dve.wait_ge(x_free[u.dest], seen.next(("mine", u.dest)))
                    if b:
                        step(V.tensor_tensor(acc[:, :, :], acc[:, :, :], acc2[:, :, :], ADD))
                    if b == 2:
                        step(V.tensor_scalar(mg_hi[:, ds(i * 2, 2), :], acc[:, :, :], 1.0, None, MUL))
                        V.tensor_tensor(mg_lo[:, ds(i * 2, 2), :], acc[:, :, :], mg_hi[:, ds(i * 2, 2), :], SUB) \
                            .then_inc(S["mg_ready"], 1)
                return go

            for name in (x_free[0], x_free[1], ada_free, S["act_ready"], S["mg_ready"]):
                dve.sem_inc(name, 1)
            V.memset(eps[:, :], EPS)
            step(V.memset(reset[:, :], 1.0))
            V.memset(reset[:, 0::128], 0.0)
            V.memset(lb[:, 0, :, :], 0.0)
            V.memset(omlb[:, 0, :, :], 1.0)
            dve.wait_ge(S["rows_turned"], 1)
            for g in range(2):
                V.tensor_copy(vec[:, :, :, g], S5[:, 0:DEPTH * V_ROWS].rearrange("p (l r) -> p l r", l=DEPTH))
            step(V.tensor_copy(misc[:, :], S5[:, 2 * V_ROWS:2 * V_ROWS + M_ROWS]))
            m_lb = misc[:, M_LB:M_LB + 16].rearrange("p (d l h) -> p d l h", d=2, l=DEPTH)
            V.tensor_tensor(lb_d[:, :, :], m_lb[:, :, 1, :], m_lb[:, :, 0, :], SUB)
            V.tensor_tensor(sub_g[:, :], misc[:, M_SUB:M_SUB + DEPTH], con[:, C_LAM + DEPTH:C_LAM + 2 * DEPTH], MUL)
            V.tensor_scalar(qn_g[:, :], misc[:, M_QN:M_QN + DEPTH], 64 ** -0.5, None, MUL)
            dve.wait_ge(S["lam_in_s"], 16)
            pairs = lam_in[:, :, :, :].rearrange("p l (a b) c -> p (l a) b c", b=2)
            step(V.tensor_tensor(lam_p[:, :, :], pairs[:, :, 0, :], pairs[:, :, 1, :], MUL))
            V.tensor_reduce(lam_s[:, :, :].rearrange("p l a -> p (l a)"), lam_p[:, :, :], AX.X, ADD) \
                .then_inc(S["vec_ready"], 1)
            dve.wait_ge(S["c_ready"], 1)
            V.tensor_tensor(c4[:, :, 2:4], c_act[:, :, :], c4[:, :, 0:2], SUB).then_inc(S["c4_ready"], 1)
            dve.wait_ge(S["c_ready"], 2)
            step(V.tensor_tensor(neg_lam[:, :], lam_s[:, :, 1], lam_s[:, :, 0], SUB))
            step(V.tensor_tensor(neg_lam[:, :], neg_lam[:, :], con[:, C_LAM:C_LAM + DEPTH], SUB))
            for b in range(NB):
                dve.wait_ge(S["x_turned"], b + 1)
                V.tensor_copy(x[:, :, b * 128:b * 128 + 128].rearrange("p (a k) t -> p a k t", a=2),
                              X[b % 2][:, :, :].rearrange("p a (k t) -> p a k t", k=4)) \
                    .then_inc(S["x_ready" if b == 2 else "x_copied"], 4 if b == 2 else 1)
            dve.wait_ge(S["mask_in"], 16)
            step(V.tensor_copy(masks[:, :, :, :], mask_f[:, :, :, :]))
            loop("first", 4, first_units(), {"mod": ada_out})
            with dve.Fori(0, DEPTH) as L:
                seen.enter("layer", L)
                pre_factors(L, 0)
                for f in range(2):
                    pre()
                    loop(f"up{f}", 11, up_units(f), {"up": up_out})
                    loop(f"down{f}", 2, down_units(f),
                         {"mod": ada_out, **{("down", j): y_out((lambda j: lambda i: i * 4 + 2 * j)(j)) for j in range(2)}}, lag=4)
                    post_factors(L, 2 * f)
                    if f == 0:
                        pre_factors(L, 1)
                        post()
                        pre()
                        loop("proj", 4, proj_units(),
                             {"mod": ada_out, **{("proj", j): proj_out((lambda j: lambda i: i * 8 + 2 * j)(j)) for j in range(4)}})
                        stream(proj_tail_units(), {("tail", j): tail_out(j) for j in range(3)}, 0)
                        mixer(L)
                        loop("merge", 4, merge_units(), {"mod": ada_out, **{("b", b): merge_out(b) for b in range(3)}})
                        loop("out", 2, out_units(),
                             {("out", j): y_out((lambda j: lambda i: i * 4 + 2 * j)(j)) for j in range(2)})
                        post_factors(L, 1)
                        pre_factors(L, 2)
                    post()
                seen.leave(DEPTH)
            for b in range(NB):
                dve.wait_ge(S["y_turned"], b + 1)
                V.tensor_copy(x_rows[:, b, :].rearrange("p (a c) -> p a c", a=2), X[b % 2][:, :, :]) \
                    .then_inc(S["y_out_ready"], 1)


def constants():
    con = np.zeros((128, C_N), np.float32)
    eye = np.eye(128, dtype=np.float32)
    con[:, C_ID:C_ID + 128] = eye
    con[:, C_ONE:C_ONE + 128] = 1.0
    i = np.arange(128)
    con[:, C_HEAD:C_HEAD + 128] = i[:, None] // 64 == i[None, :] // 64
    for m in range(128):
        if m % 32 < 16:
            con[m + 16, C_SWAP + m] = -1.0
        else:
            con[m - 16, C_SWAP + m] = 1.0
    for g in range(KVC):
        con[:, C_DUP + 128 * g:C_DUP + 128 * g + 128] = i[:, None] == 64 * g + i[None, :] % 64
    freqs = THETA ** (-np.arange(16, dtype=np.float32) / np.float32(16))
    pos = np.stack([np.arange(LAT) // GRID_W, np.arange(LAT) % GRID_W]).astype(np.float32)
    ang = pos[(i % 64) // 32] * freqs[i % 16][:, None].astype(np.float32)
    con[:, C_COS:C_COS + LAT] = np.cos(ang)
    con[:, C_SIN:C_SIN + LAT] = np.sin(ang)
    for l in range(DEPTH):
        con[:, C_LAM + l] = LAM_INIT[l]
        con[:, C_LAM + DEPTH + l] = 1.0 - LAM_INIT[l]
    masks = np.zeros((128, 2, len(LEVELS), 128), np.float32)
    for n, par in enumerate(LEVELS):
        same = i[:, None] // par == i[None, :] // par
        second = i % par >= par // 2
        masks[:, 0, n, :] = same & ~second[:, None] & second[None, :]
        masks[:, 1, n, :] = same & second[:, None] & ~second[None, :]
    return con, masks


INS = {"x_prompt": None, "x_sample": None, "c": (KT, 128), "c_ctx": (KT, 128),
       "cache_a_k": (DEPTH, PAST, 512), "cache_a_v": (DEPTH, PAST, 512), "state_hgrn": (DEPTH, 2, HB, 128, 128),
       "cache_c_k": (DEPTH, PAST, 128), "cache_c_v": (DEPTH, PAST, 128), "ada_w": None, "ffn_gate": None,
       "ffn_up": None, "ffn_down": None, "w_in": None, "diff_lambda": None, "diff_subln": None,
       "hgrn_lb": (16, 128), "hgrn_gnorm": None, "gqa_qnorm": None, "gqa_knorm": None, "w_branch_a": None,
       "w_branch_b": None, "w_branch_c": None, "w_out": None}
OUTS = {"y_prompt": (SEQ, D), "y_sample": (LAT, D), "new_a_k": (DEPTH, SEQ, 512), "new_a_v": (DEPTH, SEQ, 512),
        "new_hgrn": (DEPTH, 2, HB, 128, 128), "new_c_k": (DEPTH, SEQ, 128), "new_c_v": (DEPTH, SEQ, 128)}
SHAPES = [(1, SEQ, D), (1, LAT, D), (1, DEPTH, SEQ, HA, 128), (1, DEPTH, SEQ, HA, 128),
          (1, DEPTH, 2, HB, 128, 128), (1, DEPTH, SEQ, KVC, 64), (1, DEPTH, SEQ, KVC, 64)]


def kernel(**inputs):
    import concourse.bacc as bacc
    from concourse.bass_utils import run_bass_kernel_spmd

    arrays = {}
    for name, shape in INS.items():
        a = np.ascontiguousarray(inputs[name])
        arrays[name] = a.reshape(shape) if shape else a
    arrays["vec_rows"] = np.concatenate([np.asarray(inputs[n]).reshape(DEPTH, -1, 128)
                                         for n in ("ada_b", "norm_pre", "norm_post")], axis=1)
    arrays["consts"], arrays["masks"] = constants()

    def fresh():
        nc = bacc.Bacc("TRN2", target_bir_lowering=False, num_devices=1)
        io = {n: nc.dram_tensor(f"in_{n}", a.shape, mybir.dt.from_np(a.dtype), kind="ExternalInput").ap()
              for n, a in arrays.items()}
        out = {n: nc.dram_tensor(f"out_{n}", s, mybir.dt.float32, kind="ExternalOutput").ap() for n, s in OUTS.items()}
        return nc, io, out

    turns = {}
    nc, io, out = fresh()
    build(nc, io, out, turns, learn=True)
    nc, io, out = fresh()
    build(nc, io, out, turns)
    r = run_bass_kernel_spmd(nc, [{f"in_{n}": a for n, a in arrays.items()}], core_ids=[0])
    return tuple(r.results[0][f"out_{n}"].reshape(s) for n, s in zip(OUTS, SHAPES))
```
